# Optimizing a Trainium2 kernel written in Bass

```python
import math
import jax, jax.numpy as jnp
from jax import lax
import numpy as np

D_MODEL = 1024
BATCH = 1
SEQ = 1024
DEPTH = 1

D_MIX = 2 * D_MODEL
HG_WIDTH = D_MODEL
HG_HEAD_DIM = 128
HG_HEADS = HG_WIDTH // HG_HEAD_DIM
HG_CHUNK = 64
SSD_WIDTH = D_MIX - HG_WIDTH
SSD_HEAD_DIM = 64
SSD_HEADS = SSD_WIDTH // SSD_HEAD_DIM
SSD_GROUPS = 2
SSD_STATE = 128
SSD_CONV = 4
SSD_CHUNK = 64
SSD_CONV_DIM = SSD_WIDTH + 2 * SSD_GROUPS * SSD_STATE
IN_COLS = 4 * HG_WIDTH + SSD_WIDTH + SSD_CONV_DIM + SSD_HEADS
IN_SPLITS = (HG_WIDTH, 2 * HG_WIDTH, 3 * HG_WIDTH, 4 * HG_WIDTH,
             4 * HG_WIDTH + SSD_WIDTH, 4 * HG_WIDTH + SSD_WIDTH + SSD_CONV_DIM)
PEER_HEADS = 8
PEER_N_KEYS = 128
PEER_N_EXPERTS = PEER_N_KEYS * PEER_N_KEYS
PEER_KEY_DIM = 128
PEER_TOPK = 16
PEER_BLOCK = 128
EPS = 1e-6

kernel_name = "hymba_hgrn2_ssd_peer_block"

def rms_norm(x, w):
    xf = x.astype(jnp.float32)
    y = xf * lax.rsqrt(jnp.mean(xf * xf, axis=-1, keepdims=True) + EPS)
    return (y * w.astype(jnp.float32)).astype(x.dtype)

def causal_mask(n):
    return jnp.tril(jnp.ones((n, n), dtype=bool))

def chunk_scan(decay, chunk_states):
    def step(state, inp):
        d, s_new = inp
        return d * state + s_new, state
    init = jnp.zeros_like(chunk_states[:, 0])
    _, starts = lax.scan(step, init, (jnp.moveaxis(decay, 1, 0), jnp.moveaxis(chunk_states, 1, 0)))
    return jnp.moveaxis(starts, 0, 1)

def hgrn2_mixer(q, f_raw, i_in, g_out, lb, norm_w):
    f32 = jnp.float32
    B, S, _ = q.shape
    C = HG_CHUNK
    nc = S // C
    f = lb.astype(f32) + (1.0 - lb.astype(f32)) * jax.nn.sigmoid(f_raw.astype(f32))
    k = 1.0 - f
    logf = jnp.log(f)

    def chunks(t):
        return t.astype(f32).reshape(B, nc, C, HG_HEADS, HG_HEAD_DIM)

    qc, kc, vc, gc = chunks(q), chunks(k), chunks(i_in), chunks(logf)
    G = jnp.cumsum(gc, axis=2)
    G_last = G[:, :, -1]
    q_dec = qc * jnp.exp(G)
    k_dec = kc * jnp.exp(-G)
    scores = jnp.einsum('bcthk,bcshk->bchts', q_dec, k_dec)
    scores = jnp.where(causal_mask(C), scores, 0.0)
    o_intra = jnp.einsum('bchts,bcshv->bcthv', scores, vc)
    k_to_end = kc * jnp.exp(G_last[:, :, None] - G)
    chunk_states = jnp.einsum('bcshk,bcshv->bchkv', k_to_end, vc)
    S_starts = chunk_scan(jnp.exp(G_last)[..., None], chunk_states)
    o_inter = jnp.einsum('bcthk,bchkv->bcthv', q_dec, S_starts)
    o = (o_intra + o_inter).reshape(B, S, HG_HEADS, HG_HEAD_DIM)
    o = rms_norm(o, norm_w) * jax.nn.silu(g_out.astype(f32).reshape(B, S, HG_HEADS, HG_HEAD_DIM))
    return o.reshape(B, S, HG_WIDTH)

def ssd_mixer(z, xbc, dt_raw, conv_w, conv_b, dt_bias, A_log, D_skip, norm_w):
    f32 = jnp.float32
    B, S, _ = z.shape
    C = SSD_CHUNK
    nc = S // C
    G, Hg, P, N = SSD_GROUPS, SSD_HEADS // SSD_GROUPS, SSD_HEAD_DIM, SSD_STATE
    xbc = lax.conv_general_dilated(
        xbc.astype(f32), conv_w.astype(f32)[:, None, :], window_strides=(1,),
        padding=[(SSD_CONV - 1, 0)], dimension_numbers=('NWC', 'WIO', 'NWC'),
        feature_group_count=SSD_CONV_DIM)
    xbc = jax.nn.silu(xbc + conv_b.astype(f32))
    xs, Bm, Cm = jnp.split(xbc, [SSD_WIDTH, SSD_WIDTH + G * N], axis=-1)
    xs = xs.reshape(B, nc, C, G, Hg, P)
    Bm = Bm.reshape(B, nc, C, G, N)
    Cm = Cm.reshape(B, nc, C, G, N)
    dt = jax.nn.softplus(dt_raw.astype(f32) + dt_bias.astype(f32))
    A = -jnp.exp(A_log.astype(f32))
    dt_c = dt.reshape(B, nc, C, G, Hg)
    xdt = xs * dt_c[..., None]
    cumA = jnp.cumsum(jnp.moveaxis(dt_c * A.reshape(G, Hg), 2, -1), axis=-1)
    diff = cumA[..., :, None] - cumA[..., None, :]
    L = jnp.exp(jnp.where(causal_mask(C), diff, -jnp.inf))
    CB = jnp.einsum('bctgn,bcsgn->bcgts', Cm, Bm)
    y_diag = jnp.einsum('bcghts,bcsghp->bctghp', CB[:, :, :, None] * L, xdt)
    decay_to_end = jnp.exp(cumA[..., -1:] - cumA)
    chunk_states = jnp.einsum('bcsgn,bcghs,bcsghp->bcghpn', Bm, decay_to_end, xdt)
    S_starts = chunk_scan(jnp.exp(cumA[..., -1])[..., None, None], chunk_states)
    y_off = jnp.einsum('bctgn,bcghpn,bcght->bctghp', Cm, S_starts, jnp.exp(cumA))
    y = y_diag + y_off + D_skip.astype(f32).reshape(G, Hg, 1) * xs
    y = y.reshape(B, S, SSD_WIDTH) * jax.nn.silu(z.astype(f32))
    y = rms_norm(y.reshape(B, S, G, SSD_WIDTH // G), norm_w.reshape(G, SSD_WIDTH // G))
    return y.reshape(B, S, SSD_WIDTH)

def peer_ffn(h, w_q, keys, u, v):
    f32 = jnp.float32
    B, S, D = h.shape
    K = PEER_TOPK
    blocks = h.reshape((B * S) // PEER_BLOCK, PEER_BLOCK, D)

    def block_fn(xb):
        q = (xb @ w_q).reshape(PEER_BLOCK, PEER_HEADS, 2, PEER_KEY_DIM)
        sc = jnp.einsum('thpd,hpkd->thpk', q, keys).astype(f32)
        top_v, top_i = lax.top_k(sc, K)
        cand = (top_v[:, :, 0, :, None] + top_v[:, :, 1, None, :]).reshape(PEER_BLOCK, PEER_HEADS, K * K)
        best_v, best_i = lax.top_k(cand, K)
        i1 = jnp.take_along_axis(top_i[:, :, 0], best_i // K, axis=-1)
        i2 = jnp.take_along_axis(top_i[:, :, 1], best_i % K, axis=-1)
        experts = (i1 * PEER_N_KEYS + i2).reshape(PEER_BLOCK, PEER_HEADS * K)
        gate = jax.nn.softmax(best_v, axis=-1).reshape(PEER_BLOCK, PEER_HEADS * K)
        u_sel = u[experts]
        v_sel = v[experts]
        act = jax.nn.gelu(jnp.einsum('ted,td->te', u_sel, xb).astype(f32), approximate=False) * gate
        return jnp.einsum('te,ted->td', act.astype(v_sel.dtype), v_sel)

    out = lax.map(block_fn, blocks)
    return out.reshape(B, S, D)

def setup_inputs(seed: int = 0) -> dict:
    key = jax.random.key(seed)
    ks = jax.random.split(key, 18)
    f32 = jnp.float32
    Ld = DEPTH

    def nrm(k, shape, scale):
        return jax.random.normal(k, shape, f32) * scale

    dt0 = jnp.exp(jax.random.uniform(ks[7], (Ld, SSD_HEADS), f32, math.log(1e-3), math.log(1e-1)))
    return {
        "x": nrm(ks[0], (BATCH, SEQ, D_MODEL), 1.0),
        "norm_mix_w": 1.0 + nrm(ks[1], (Ld, D_MODEL), 0.02),
        "w_in": nrm(ks[2], (Ld, D_MODEL, IN_COLS), D_MODEL ** -0.5),
        "hg_lb_logits": nrm(ks[3], (Ld + 1, HG_WIDTH), 0.1),
        "hg_norm_w": 1.0 + nrm(ks[4], (Ld, HG_HEAD_DIM), 0.02),
        "ssd_conv_w": nrm(ks[5], (Ld, SSD_CONV, SSD_CONV_DIM), SSD_CONV ** -0.5),
        "ssd_conv_b": nrm(ks[6], (Ld, SSD_CONV_DIM), 0.02),
        "ssd_dt_bias": dt0 + jnp.log(-jnp.expm1(-dt0)),
        "ssd_A_log": jnp.log(jax.random.uniform(ks[8], (Ld, SSD_HEADS), f32, 1.0, 16.0)),
        "ssd_D": 1.0 + nrm(ks[9], (Ld, SSD_HEADS), 0.1),
        "ssd_norm_w": 1.0 + nrm(ks[10], (Ld, SSD_WIDTH), 0.02),
        "w_out": nrm(ks[11], (Ld, D_MIX, D_MODEL), D_MIX ** -0.5),
        "norm_ffn_w": 1.0 + nrm(ks[12], (Ld, D_MODEL), 0.02),
        "peer_w_q": nrm(ks[13], (Ld, D_MODEL, PEER_HEADS * 2 * PEER_KEY_DIM), D_MODEL ** -0.5),
        "peer_keys": nrm(ks[14], (Ld, PEER_HEADS, 2, PEER_N_KEYS, PEER_KEY_DIM), PEER_KEY_DIM ** -0.5),
        "peer_u": nrm(ks[15], (Ld, PEER_N_EXPERTS, D_MODEL), D_MODEL ** -0.5),
        "peer_v": nrm(ks[16], (Ld, PEER_N_EXPERTS, D_MODEL), PEER_HEADS ** -0.5),
        "final_norm_w": 1.0 + nrm(ks[17], (D_MODEL,), 0.02),
    }

def reference(x, norm_mix_w, w_in, hg_lb_logits, hg_norm_w, ssd_conv_w, ssd_conv_b,
              ssd_dt_bias, ssd_A_log, ssd_D, ssd_norm_w, w_out, norm_ffn_w,
              peer_w_q, peer_keys, peer_u, peer_v, final_norm_w):
    lbs = jnp.cumsum(jax.nn.softmax(hg_lb_logits.astype(jnp.float32), axis=0), axis=0)
    for l in range(DEPTH):
        h = rms_norm(x, norm_mix_w[l])
        proj = h @ w_in[l]
        q, f_raw, i_in, g_out, z, xbc, dt_raw = jnp.split(proj, IN_SPLITS, axis=-1)
        o_hg = hgrn2_mixer(q, f_raw, i_in, g_out, lbs[l], hg_norm_w[l])
        o_ssd = ssd_mixer(z, xbc, dt_raw, ssd_conv_w[l], ssd_conv_b[l], ssd_dt_bias[l],
                          ssd_A_log[l], ssd_D[l], ssd_norm_w[l])
        mixed = jnp.concatenate([o_hg, o_ssd], axis=-1).astype(x.dtype)
        x = x + mixed @ w_out[l]
        x = x + peer_ffn(rms_norm(x, norm_ffn_w[l]), peer_w_q[l], peer_keys[l], peer_u[l], peer_v[l])
    return rms_norm(x, final_norm_w)


_drawn_inputs = setup_inputs


def setup_inputs(seed=0):
    import zlib

    import numpy as np

    out = dict(_drawn_inputs(seed))
    spreads = {}
    factors = {'hg_norm_w': 13.319, 'ssd_norm_w': 8.744, 'norm_ffn_w': 8.609, 'final_norm_w': 8.236}
    for name, (base, spread) in spreads.items():
        noise = np.random.default_rng([zlib.crc32(name.encode()), seed]).standard_normal(out[name].shape)
        drawn = base * np.exp(spread * noise) if base else spread * noise
        out[name] = __import__('jax').numpy.asarray(drawn.astype(out[name].dtype))
    for name, factor in factors.items():
        out[name] = (out[name] * factor).astype(out[name].dtype)
    return out
```

```python
from contextlib import ExitStack

import concourse.bass as bass
from concourse import mybir

F32 = mybir.dt.float32
U32 = mybir.dt.uint32
ALU = mybir.AluOpType
ACT = mybir.ActivationFunctionType
AX_X = mybir.AxisListType.X

P = 128
T = 1024
NB = T // P
D = 1024
KT = D // P
C = 64
NC = T // C
HG_HEADS = 8
SSD_HEADS = 16
SSD_P = 64
CT = 12
MT = 16
TAPS = 4
PH = 8
K = 16
NK = 128
EPS = 1e-6
LOWEST = -3.0e38
RING = 8
PAIR = 2


class Sems(dict):

    def __init__(self, ctx, nc):
        self.ctx, self.nc = ctx, nc

    def __missing__(self, name):
        self[name] = self.ctx.enter_context(self.nc.semaphore(name))
        return self[name]


def seg(region, start, *shape):
    size = 1
    for n in shape:
        size *= n
    ap = region[:, start:start + size]
    if len(shape) == 2:
        ap = ap.rearrange("p (a b) -> p a b", a=shape[0])
    elif len(shape) == 3:
        ap = ap.rearrange("p (a b c) -> p a b c", a=shape[0], b=shape[1])
    return ap


def first(n):
    return isinstance(n, int) and n == 0


def layer(nc, io):
    with ExitStack() as ctx:
        def sb(name, shape, dt=F32):
            return ctx.enter_context(nc.sbuf_tensor(name, shape, dt))

        m = {
            "A": sb("region_a", [P, 8192]),
            "B": sb("region_b", [P, 16384]),
            "C": sb("region_c", [P, 8192]),
            "D": sb("region_d", [P, 17408]),
            "ps": ctx.enter_context(nc.psum_tensor("ps", [P, 8, 512], F32)),
            "ident": sb("ident", [P, P]),
            "mask": sb("mask", [P, P], U32),
            "keep": sb("keep", [P, T]),
            "nrow": sb("nrow", [P, D]),
            "col": sb("col", [P, 160]),
            "ss": sb("ss", [P, 32]),
            "u32": (sb("top_i", [P, 2, K], U32), sb("best_i", [P, K], U32), sb("place", [P, 2, K], U32),
                    sb("ids", [P, NB, K], U32)),
        }
        s = Sems(ctx, nc)
        norm_in(nc, m, s, io)
        project_v(nc, m, s, io)
        hgrn(nc, m, s, io)
        project_z(nc, m, s, io)
        project_xbc(nc, m, s, io)
        ssd(nc, m, s, io)
        project_out(nc, m, s, io)
        norm_ffn(nc, m, s, io)
        peer(nc, m, s, io)
        norm_final(nc, m, s, io)


LBL = 0
LB = 16
OMLB = 24
HGW = 32
CONVW = 33
CONVB = 81
SSDW = 93
SSDH = 101
DROW = 104
IOTA = 120
TMP = 136


def norm_blocks(nc, block, m, s, before, src, dst, dst_t, junk, ready):
    ps, ss = m["ps"], m["ss"]
    sq, mean, root, rstd, normed, turned, stored = (s[n] for n in (
        "squared", "mean", "root", "rstd", "normed", "turned", "stored"))

    @block.scalar
    def _(act):
        act.wait_ge(*ready)
        for b in range(NB):
            if b >= 1:
                act.wait_ge(sq, before + b)
            nc.scalar.activation(junk, src[:, b, :], ACT.Square, accum_out=ss[:, b:b + 1]).then_inc(sq, 1)
        act.wait_ge(mean, before // NB + 1)
        nc.scalar.activation(ss[:, 8:16], ss[:, 8:16], ACT.Sqrt).then_inc(root, 1)
        for b in range(NB):
            act.wait_ge(turned, before + b + 1)
            nc.scalar.copy(dst_t[:, :, b * P:(b + 1) * P],
                           ps[:, 2 * (b % 2):2 * (b % 2) + 2, :].rearrange("p u (k t) -> p (u k) t", k=4)
                           ).then_inc(stored, 1)

    @block.vector
    def _(dve):
        dve.wait_ge(*ready)
        dve.wait_ge(sq, before + NB)
        nc.vector.tensor_scalar(ss[:, 8:16], ss[:, 0:8], 1.0 / D, EPS, ALU.mult, ALU.add).then_inc(mean, 1)
        dve.wait_ge(root, before // NB + 1)
        nc.vector.reciprocal(ss[:, 16:24], ss[:, 8:16]).then_inc(rstd, 1)
        dve.wait_ge(rstd, before // NB + 1)
        for b in range(NB):
            nc.vector.scalar_tensor_tensor(out=dst[:, b, :], in0=src[:, b, :], scalar=ss[:, 16 + b:17 + b],
                                           in1=m["nrow"][:], op0=ALU.mult, op1=ALU.mult).then_inc(normed, 1)

    @block.tensor
    def _(pe):
        for b in range(NB):
            pe.wait_ge(normed, before + b + 1)
            if b >= 2:
                pe.wait_ge(stored, before + b - 1)
            for k in range(KT):
                last = nc.tensor.transpose(ps[:, 2 * (b % 2) + k // 4, (k % 4) * P:(k % 4 + 1) * P],
                                           dst[:, b, k * P:(k + 1) * P], m["ident"][:])
            last.then_inc(turned, 1)


def norm_in(nc, m, s, io):
    x_all = seg(m["C"], 0, NB, D)
    h_t = seg(m["A"], 0, KT, T)
    with nc.Block() as block:
        @block.sync
        def _(sp):
            sp.dma_start(m["nrow"][:], io["norm_mix_row"]).then_inc(s["x_loaded"], 16)
            sp.dma_start(m["ident"][:], io["ident"]).then_inc(s["x_loaded"], 16)
            sp.dma_start(x_all, io["x"].rearrange("(b p) d -> p b d", p=P)).then_inc(s["x_loaded"], 16)
            sp.dma_start(m["col"][:, 0:TMP], io["cols"]).then_inc(s["consts"], 16)
            sp.dma_start(m["mask"][:], io["mask"]).then_inc(s["consts"], 16)
            sp.dma_start(m["keep"][:], io["keep"]).then_inc(s["consts"], 16)
            for c in range(2):
                sp.dma_start(seg(m["D"], 4096 * c, 4096), io["w_v"][c]).then_inc(s[f"half_w{c}"], 16)
            sp.wait_ge(s["x_loaded"], 48)
            sp.sem_inc(s["x_here"], 1)

        norm_blocks(nc, block, m, s, 0, x_all, x_all, h_t, m["B"][:, 0:D], (s["x_here"], 1))


def natural_groups(nc, pe, m, s, lhs, rhs, tiles, use, psum_free, banks):
    n = 0
    for c in range(2):
        pe.wait_ge(s[f"half_w{c}"], 16 * (use + 1))
        for b in range(NB):
            if n >= banks:
                pe.wait_ge(s[psum_free], n - banks + 1)
            for k in range(tiles):
                last = nc.tensor.matmul(m["ps"][:, n % banks, :], lhs[:, k, b * P:(b + 1) * P],
                                        rhs[c][:, k * 512:(k + 1) * 512], start=(k == 0), stop=(k == tiles - 1))
            last.then_inc(s["half_psum"], 1)
            n += 1


def project_v(nc, m, s, io):
    h_t = seg(m["A"], 0, KT, T)
    v = seg(m["C"], 0, NB, D)
    col = m["col"]
    with nc.Block() as block:
        @block.sync
        def _(sp):
            sp.dma_start(seg(m["D"], 8192, 2048), io["w_hg"][0, :, 0:2048]).then_inc(s["w_fg"], 16)
            sp.dma_start(seg(m["D"], 10240, 1024), io["w_hg"][0, :, 2048:3072]).then_inc(s["w_q"], 16)

        @block.tensor
        def _(pe):
            natural_groups(nc, pe, m, s, h_t, [seg(m["D"], 4096 * c, 4096) for c in range(2)], KT,
                           0, "v_stored", 4)

        @block.scalar
        def _(act):
            act.wait_ge(s["lb_max"], 2)
            nc.scalar.activation(col[:, TMP:TMP + 16], col[:, LBL:LBL + 16], ACT.Exp).then_inc(s["lb_exp"], 1)
            for n in range(16):
                act.wait_ge(s["half_psum"], n + 1)
                nc.scalar.copy(v[:, n % NB, (n // NB) * 512:(n // NB + 1) * 512],
                               m["ps"][:, n % 4, :]).then_inc(s["v_stored"], 1)

        @block.vector
        def _(dve):
            dve.wait_ge(s["consts"], 48)
            nc.vector.tensor_tensor(col[:, TMP:TMP + 8], col[:, LBL:LBL + 8], col[:, LBL + 8:LBL + 16],
                                    ALU.max).then_inc(s["lb_max0"], 1)
            dve.wait_ge(s["lb_max0"], 1)
            for r in range(2):
                nc.vector.tensor_tensor(col[:, LBL + 8 * r:LBL + 8 * r + 8], col[:, LBL + 8 * r:LBL + 8 * r + 8],
                                        col[:, TMP:TMP + 8], ALU.subtract).then_inc(s["lb_max"], 1)
            dve.wait_ge(s["lb_exp"], 1)
            nc.vector.tensor_tensor(col[:, LB:LB + 8], col[:, TMP:TMP + 8], col[:, TMP + 8:TMP + 16],
                                    ALU.add).then_inc(s["lb_step"], 1)
            dve.wait_ge(s["lb_step"], 1)
            nc.vector.reciprocal(col[:, OMLB:OMLB + 8], col[:, LB:LB + 8]).then_inc(s["lb_step"], 1)
            dve.wait_ge(s["lb_step"], 2)
            nc.vector.tensor_tensor(col[:, LB:LB + 8], col[:, TMP:TMP + 8], col[:, OMLB:OMLB + 8],
                                    ALU.mult).then_inc(s["lb_step"], 1)
            dve.wait_ge(s["lb_step"], 3)
            nc.vector.tensor_scalar(col[:, OMLB:OMLB + 8], col[:, LB:LB + 8], -1.0, 1.0, ALU.mult, ALU.add)


def hgrn(nc, m, s, io):
    h_t = seg(m["A"], 0, KT, T)
    v = seg(m["C"], 0, NB, HG_HEADS, P)
    mixed_t = seg(m["B"], 0, MT, T)
    w = seg(m["D"], 8192, 3, KT, P)
    f = seg(m["D"], 0, T)
    k = seg(m["D"], 1024, T)
    silu_g = seg(m["D"], 2048, T)
    G = seg(m["D"], 3072, T)
    eG = seg(m["D"], 4096, T)
    k_dec = seg(m["D"], 5120, T)
    k_end = seg(m["D"], 6144, T)
    q_dec = seg(m["D"], 7168, T)
    v_head = seg(m["D"], 11264, NB, P)
    o_normed = seg(m["D"], 12288, NB, P)
    k_nat = seg(m["D"], 13312, NB, P)
    scores = seg(m["D"], 14336, NB, P)
    state = seg(m["D"], 15360, NC, P)
    junk = seg(m["D"], 6144, NB, P)
    STEPS = NC - 1
    ps = m["ps"]
    col, ss = m["col"], m["ss"]
    fq_ps = ps[:, 0:2, :].rearrange("p a b -> p (a b)")
    g_ps = ps[:, 2:4, :].rearrange("p a b -> p (a b)")
    o_ps = ps[:, 4:6, :].rearrange("p u (b x) -> p (u b) x", b=4)
    oT_ps = ps[:, 4:6, :].rearrange("p a b -> p (a b)")

    def block_ps(bank, b):
        return ps[:, bank + b // 4, (b % 4) * P:(b % 4 + 1) * P]

    def sum_ps(j):
        return ps[:, 4 + j % 2 * 2 + j // 8, (j // 2 % 4) * P:(j // 2 % 4 + 1) * P]

    def bank_ps(bank):
        return ps[:, bank, :].rearrange("p (b x) -> p b x", b=4)

    def by_chunk(ap):
        return ap.rearrange("p (c t) -> p c t", t=C)

    with nc.Block() as block:
        @block.sync
        def _(sp):
            with sp.Fori(0, HG_HEADS - 1) as h:
                sp.wait_ge(s["g_psum"], h + 1)
                sp.dma_start(seg(m["D"], 8192, 2048), io["w_hg"][bass.ds(h + 1, 1), :, 0:2048].rearrange(
                    "a p n -> p (a n)")).then_inc(s["w_fg"], 16)
                sp.wait_ge(s["q_psum"], h + 1)
                sp.dma_start(seg(m["D"], 10240, 1024), io["w_hg"][bass.ds(h + 1, 1), :, 2048:3072].rearrange(
                    "a p n -> p (a n)")).then_inc(s["w_q"], 16)

        @block.gpsimd
        def _(pool):
            def take_v(h):
                if not first(h):
                    pool.wait_ge(s["o_psum"], 2 * h)
                    pool.sem_inc(s["pool_gate"], 1)
                nc.gpsimd.tensor_copy(v_head, v[:, :, bass.ds(h, 1), :].rearrange("p b a x -> p b (a x)")
                                      ).then_inc(s["v_head"], 1)
            take_v(0)
            with pool.Fori(1, HG_HEADS) as h:
                take_v(h)

        @block.tensor
        def _(pe):
            def product(dst, which):
                for u in range(2):
                    for kt in range(KT):
                        last = nc.tensor.matmul(dst[:, u * 512:(u + 1) * 512], w[:, which, kt, :],
                                                h_t[:, kt, u * 512:(u + 1) * 512], start=(kt == 0), stop=(kt == KT - 1))
                return last

            def project_fg(h):
                pe.wait_ge(s["w_fg"], 16 * (h + 1))
                if not first(h):
                    pe.wait_ge(s["q_dec"], h)
                product(fq_ps, 0).then_inc(s["f_psum"], 1)
                if not first(h):
                    pe.wait_ge(s["silu_g"], h)
                product(g_ps, 1).then_inc(s["g_psum"], 1)

            def project_q(h):
                pe.wait_ge(s["w_q"], 16 * (h + 1))
                pe.wait_ge(s["f_sig"], h + 1)
                product(fq_ps, 2).then_inc(s["q_psum"], 1)

            def attend(h):
                pe.wait_ge(s["q_dec"], h + 1)
                pe.wait_ge(s["k_dec"], h + 1)
                if not first(h):
                    pe.wait_ge(s["mixed"], h)
                for b in range(NB):
                    last = nc.tensor.matmul(block_ps(4, b), k_dec[:, b * P:(b + 1) * P],
                                            q_dec[:, b * P:(b + 1) * P], start=True, stop=True)
                last.then_inc(s["scores_psum"], 1)
                pe.wait_ge(s["k_end"], h + 1)
                for b in range(NB):
                    last = nc.tensor.transpose(block_ps(6, b), k_end[:, b * P:(b + 1) * P], m["ident"][:])
                last.then_inc(s["k_nat_psum"], 1)
                pe.wait_ge(s["v_head"], h + 1)
                pe.wait_ge(s["k_nat"], h + 1)
                pe.wait_ge(s["scores"], 2 * h + 2)
                for j in range(STEPS):
                    b, rows = j // 2, slice(j % 2 * C, (j % 2 + 1) * C)
                    last = nc.tensor.matmul(sum_ps(j), k_nat[rows, b, :], v_head[rows, b, :], start=True, stop=True)
                    if j == 7 or j == STEPS - 1:
                        last.then_inc(s["sums_psum"], 1)
                pe.wait_ge(s["state_zero"], 1)
                for b in range(NB):
                    if b % 4 == 0:
                        pe.wait_ge(s["state"], STEPS * h + (8 if b == 0 else STEPS))
                    nc.tensor.matmul(o_ps[:, b, :], scores[:, b, :], v_head[:, b, :], start=True, stop=False,
                                     skip_group_check=True)
                    for c in range(2):
                        j = 2 * b + c
                        last = nc.tensor.matmul(o_ps[c * C:(c + 1) * C, b, :], q_dec[:, j * C:(j + 1) * C],
                                                state[:, j, :], start=False, stop=True, skip_group_check=True)
                    if b % 4 == 3:
                        last.then_inc(s["o_psum"], 1)

            def turn(h):
                pe.wait_ge(s["o_normed"], h + 1)
                for b in range(NB):
                    last = nc.tensor.transpose(oT_ps[:, b * P:(b + 1) * P], o_normed[:, b, :], m["ident"][:])
                last.then_inc(s["oT_psum"], 1)

            project_fg(0)
            project_q(0)
            with pe.Fori(0, HG_HEADS - 1) as h:
                project_fg(h + 1)
                attend(h)
                project_q(h + 1)
                turn(h)
            attend(HG_HEADS - 1)
            turn(HG_HEADS - 1)

        @block.scalar
        def _(act):
            def head(h):
                act.wait_ge(s["f_psum"], h + 1)
                if not first(h):
                    act.wait_ge(s["G"], h)
                nc.scalar.activation(f, fq_ps, ACT.Sigmoid).then_inc(s["f_sig"], 1)
                act.wait_ge(s["g_psum"], h + 1)
                if not first(h):
                    act.wait_ge(s["mixed"], h)
                nc.scalar.activation(silu_g, g_ps, ACT.Sigmoid).then_inc(s["g_sig"], 1)
                act.wait_ge(s["f"], h + 1)
                act.wait_ge(s["k"], h + 1)
                nc.scalar.activation(f, f, ACT.Ln).then_inc(s["log_f"], 1)
                act.wait_ge(s["G"], h + 1)
                if not first(h):
                    act.wait_ge(s["state"], STEPS * h)
                nc.scalar.activation(eG, G, ACT.Exp).then_inc(s["eG"], 1)
                if not first(h):
                    act.wait_ge(s["scores_psum"], h)
                nc.scalar.activation(k_dec, G, ACT.Exp, scale=-1.0).then_inc(s["emG"], 1)
                act.wait_ge(s["to_end"], h + 1)
                nc.scalar.activation(k_end, k_end, ACT.Exp).then_inc(s["e_end"], 1)
                act.wait_ge(s["k_nat_psum"], h + 1)
                if not first(h):
                    act.wait_ge(s["sums_psum"], 2 * h)
                nc.scalar.copy(k_nat, ps[:, 6:8, :].rearrange("p u (b x) -> p (u b) x", b=4)).then_inc(s["k_nat"], 1)
                for b in range(NB):
                    if b % 4 == 0:
                        act.wait_ge(s["o_psum"], 2 * h + b // 4 + 1)
                    nc.scalar.activation(junk[:, b, :], o_ps[:, b, :], ACT.Square, accum_out=ss[:, b:b + 1]
                                         ).then_inc(s["o_squared"], 1)
                act.wait_ge(s["o_mean"], h + 1)
                nc.scalar.activation(ss[:, 8:16], ss[:, 8:16], ACT.Sqrt).then_inc(s["o_root"], 1)

            head(0)
            with act.Fori(1, HG_HEADS) as h:
                head(h)

        @block.vector
        def _(dve):
            nc.vector.memset(scores, 0.0).then_inc(s["scores_zero"], 1)
            nc.vector.memset(state[:, 0, :], 0.0).then_inc(s["state_zero"], 1)
            dve.wait_ge(s["scores_zero"], 1)

            def head(h):
                lb = col[:, bass.ds(h + LB, 1)]
                omlb = col[:, bass.ds(h + OMLB, 1)]
                dve.wait_ge(s["f_sig"], h + 1)
                nc.vector.tensor_scalar(f, f, omlb, lb, ALU.mult, ALU.add).then_inc(s["f"], 1)
                dve.wait_ge(s["f"], h + 1)
                nc.vector.tensor_scalar(k, f, -1.0, 1.0, ALU.mult, ALU.add).then_inc(s["k"], 1)
                dve.wait_ge(s["g_sig"], h + 1)
                nc.vector.tensor_tensor(silu_g, silu_g, g_ps, ALU.mult).then_inc(s["silu_g"], 1)
                dve.wait_ge(s["log_f"], h + 1)
                nc.vector.tensor_tensor_scan(G, m["keep"][:], f, 0.0, ALU.mult, ALU.add).then_inc(s["G"], 1)
                dve.wait_ge(s["G"], h + 1)
                if not first(h):
                    dve.wait_ge(s["k_nat_psum"], h)
                nc.vector.tensor_tensor(by_chunk(k_end), by_chunk(G)[:, :, C - 1:C].to_broadcast([P, NC, C]),
                                        by_chunk(G), ALU.subtract).then_inc(s["to_end"], 1)
                dve.wait_ge(s["eG"], h + 1)
                dve.wait_ge(s["q_psum"], h + 1)
                if not first(h):
                    dve.wait_ge(s["o_psum"], 2 * h)
                nc.vector.tensor_tensor(q_dec, eG, fq_ps, ALU.mult).then_inc(s["q_dec"], 1)
                dve.wait_ge(s["emG"], h + 1)
                nc.vector.tensor_tensor(k_dec, k_dec, k, ALU.mult).then_inc(s["k_dec"], 1)
                dve.wait_ge(s["e_end"], h + 1)
                nc.vector.tensor_tensor(k_end, k_end, k, ALU.mult).then_inc(s["k_end"], 1)
                dve.wait_ge(s["scores_psum"], h + 1)
                dve.sem_inc(s["dve_gate"], 1)
                for u in range(2):
                    nc.vector.copy_predicated(scores[:, 4 * u:4 * u + 4, :],
                                              m["mask"][:].unsqueeze(1).to_broadcast([P, 4, P]), bank_ps(4 + u)
                                              ).then_inc(s["scores"], 1)
                for j in range(STEPS):
                    if j % 8 == 0:
                        dve.wait_ge(s["sums_psum"], 2 * h + j // 8 + 1)
                    if j > 0:
                        dve.wait_ge(s["state"], STEPS * h + j)
                    nc.vector.scalar_tensor_tensor(
                        out=state[:, j + 1, :], in0=state[:, j, :], scalar=eG[:, j * C + C - 1:j * C + C],
                        in1=sum_ps(j), op0=ALU.mult, op1=ALU.add
                        ).then_inc(s["state"], 1)
                dve.wait_ge(s["o_squared"], NB * (h + 1))
                nc.vector.tensor_scalar(ss[:, 8:16], ss[:, 0:8], 1.0 / P, EPS, ALU.mult, ALU.add).then_inc(s["o_mean"], 1)
                dve.wait_ge(s["o_root"], h + 1)
                nc.vector.reciprocal(ss[:, 16:24], ss[:, 8:16]).then_inc(s["o_rstd"], 1)
                dve.wait_ge(s["o_rstd"], h + 1)
                nc.vector.tensor_tensor(o_normed, o_ps, ss[:, 16:24].unsqueeze(2).to_broadcast([P, NB, P]),
                                        ALU.mult).then_inc(s["o_normed"], 1)
                dve.wait_ge(s["oT_psum"], h + 1)
                nc.vector.scalar_tensor_tensor(
                    out=mixed_t[:, bass.ds(h, 1), :].rearrange("p a t -> p (a t)"), in0=oT_ps,
                    scalar=col[:, HGW:HGW + 1], in1=silu_g, op0=ALU.mult, op1=ALU.mult).then_inc(s["mixed"], 1)
            head(0)
            with dve.Fori(1, HG_HEADS) as h:
                head(h)


def project_z(nc, m, s, io):
    h_t = seg(m["A"], 0, KT, T)
    z = seg(m["C"], 0, NB, D)
    with nc.Block() as block:
        @block.sync
        def _(sp):
            for c in range(2):
                sp.dma_start(seg(m["B"], 8192 + 4096 * c, 4096), io["w_z"][c]).then_inc(s[f"half_w{c}"], 16)
            for u in range(2):
                sp.dma_start(seg(m["D"], 12288 + 1024 * u, 1024), io["w_xbc"][u]).then_inc(s[f"w_xbc{u}"], 16)

        @block.tensor
        def _(pe):
            natural_groups(nc, pe, m, s, h_t, [seg(m["B"], 8192 + 4096 * c, 4096) for c in range(2)], KT,
                           1, "z_stored", 4)

        @block.scalar
        def _(act):
            for n in range(16):
                act.wait_ge(s["half_psum"], 16 + n + 1)
                nc.scalar.activation(z[:, n % NB, (n // NB) * 512:(n // NB + 1) * 512], m["ps"][:, n % 4, :],
                                     ACT.Sigmoid).then_inc(s["z_sig"], 1)

        @block.vector
        def _(dve):
            for n in range(16):
                part = z[:, n % NB, (n // NB) * 512:(n // NB + 1) * 512]
                dve.wait_ge(s["z_sig"], n + 1)
                nc.vector.tensor_tensor(part, part, m["ps"][:, n % 4, :], ALU.mult).then_inc(s["z_stored"], 1)


XBC = 0
SEL = 12288
SSN = 14336
DECAY = 14848
CUM = 15104


def project_xbc(nc, m, s, io):
    h_t = seg(m["A"], 0, KT, T)
    xbc = seg(m["D"], XBC, CT, T)
    w = [seg(m["D"], SEL + 1024 * u, KT, P) for u in range(2)]
    raw = [seg(m["B"], 8192 + 1027 * u, TAPS - 1 + T) for u in range(2)]
    sig = seg(m["B"], 10246, T)
    w_dt = seg(m["B"], 11270, KT, SSD_HEADS)
    H = SSD_HEADS
    dt, t1, eC = (m["B"][0:H, 11398 + 1024 * u:12422 + 1024 * u] for u in range(3))
    diag = m["B"][0:H, 14470:14726].rearrange("p (c h) -> p c h", h=H)
    ones = m["B"][0:H, 14726:14854]
    cum = m["D"][0:H, CUM:CUM + T]
    col, ps, keep = m["col"], m["ps"], m["keep"]
    dt_ps = ps[0:H, 4:6, :].rearrange("p a b -> p (a b)")

    def by_chunk(ap):
        return ap.rearrange("p (c t) -> p c t", t=C)

    with nc.Block() as block:
        @block.sync
        def _(sp):
            sp.dma_start(seg(m["B"], 11270, KT * H), io["w_dt"]).then_inc(s["w_dt"], 16)
            with sp.Fori(0, CT // 2 - 1) as i:
                for u in range(2):
                    sp.wait_ge(s["xbc_psum"], 2 * i + u + 1)
                    sp.dma_start(seg(m["D"], SEL + 1024 * u, 1024), io["w_xbc"][bass.ds(2 * i + u + 2, 1)].rearrange(
                        "a p n -> p (a n)")).then_inc(s[f"w_xbc{u}"], 16)

        @block.tensor
        def _(pe):
            pe.wait_ge(s["w_dt"], 16)
            for u in range(2):
                for kt in range(KT):
                    last = nc.tensor.matmul(dt_ps[:, u * 512:(u + 1) * 512], w_dt[:, kt, :],
                                            h_t[:, kt, u * 512:(u + 1) * 512], start=(kt == 0), stop=(kt == KT - 1))
            last.then_inc(s["dt_psum"], 1)

            def tile(i, u):
                n = 2 * i + u
                pe.wait_ge(s[f"w_xbc{u}"], 16 * (i + 1))
                if not first(i):
                    pe.wait_ge(s["raw"], n - 1)
                for t in range(2):
                    for kt in range(KT):
                        last = nc.tensor.matmul(ps[:, 2 * u + t, :], w[u][:, kt, :], h_t[:, kt, t * 512:(t + 1) * 512],
                                                start=(kt == 0), stop=(kt == KT - 1))
                last.then_inc(s["xbc_psum"], 1)

            tile(0, 0)
            tile(0, 1)
            for q, (rows, ready, count) in enumerate(((dt, "dt", 1), (cum, "cum", 1), (eC, "eC", 1), (t1, "dt_end", 1))):
                pe.wait_ge(s[ready], count)
                for b in range(NB):
                    last = nc.tensor.transpose(ps[:, 6, (4 * b + q) * H:(4 * b + q + 1) * H],
                                               rows[:, b * P:(b + 1) * P], m["ident"][0:H, 0:H])
            last.then_inc(s["nat_psum"], 1)
            pe.wait_ge(s["diag"], 1)
            pe.wait_ge(s["ones"], 1)
            nc.tensor.matmul(ps[:, 7, 0:NC * H], ones, m["B"][0:H, 14470:14726], start=True, stop=True
                             ).then_inc(s["decay_psum"], 1)
            with pe.Fori(1, CT // 2) as i:
                tile(i, 0)
                tile(i, 1)

        @block.scalar
        def _(act):
            act.wait_ge(s["dt_abs"], 1)
            nc.scalar.activation(t1, t1, ACT.Exp, scale=-1.0).then_inc(s["dt_exp"], 1)
            act.wait_ge(s["dt_exp"], 1)
            nc.scalar.activation(t1, t1, ACT.Ln, bias=1.0).then_inc(s["dt_log"], 1)
            nc.scalar.activation(col[0:H, SSDH + 2:SSDH + 3], col[0:H, SSDH + 1:SSDH + 2], ACT.Exp).then_inc(s["A_exp"], 1)
            act.wait_ge(s["cum"], 1)
            nc.scalar.activation(eC, cum, ACT.Exp).then_inc(s["eC"], 1)
            act.wait_ge(s["c_end"], 1)
            nc.scalar.activation(t1, t1, ACT.Exp).then_inc(s["e_c_end"], 1)
            act.wait_ge(s["nat_psum"], 1)
            nc.scalar.copy(seg(m["D"], SSN, 512), ps[:, 6, :])
            act.wait_ge(s["decay_psum"], 1)
            nc.scalar.copy(seg(m["D"], DECAY, 256), ps[:, 7, 0:256])

            def tile(i, u):
                n = 2 * i + u
                act.wait_ge(s["xbc_psum"], n + 1)
                if not first(i):
                    act.wait_ge(s["conv"], TAPS * (n - 1))
                nc.scalar.copy(raw[u][:, TAPS - 1:], ps[:, 2 * u:2 * u + 2, :].rearrange("p a b -> p (a b)")
                               ).then_inc(s["raw"], 1)
                act.wait_ge(s["conv"], TAPS * (n + 1))
                if not (first(i) and u == 0):
                    act.wait_ge(s["xbc"], n)
                nc.scalar.activation(sig, xbc[:, bass.ds(n, 1), :].rearrange("p a t -> p (a t)"), ACT.Sigmoid
                                     ).then_inc(s["xbc_sig"], 1)
            tile(0, 0)
            tile(0, 1)
            with act.Fori(1, CT // 2) as i:
                tile(i, 0)
                tile(i, 1)

        @block.vector
        def _(dve):
            for u in range(2):
                nc.vector.memset(raw[u][:, 0:TAPS - 1], 0.0).then_inc(s["raw_zero"], 1)
            nc.vector.memset(ones, 1.0).then_inc(s["ones"], 1)
            dve.wait_ge(s["dt_psum"], 1)
            nc.vector.tensor_scalar(dt, dt_ps, col[0:H, SSDH:SSDH + 1], None, ALU.add).then_inc(s["dt_raw"], 1)
            dve.wait_ge(s["dt_raw"], 1)
            nc.vector.scalar_tensor_tensor(out=t1, in0=dt, scalar=-1.0, in1=dt, op0=ALU.mult, op1=ALU.max).then_inc(s["dt_abs"], 1)
            dve.wait_ge(s["dt_log"], 1)
            nc.vector.scalar_tensor_tensor(out=dt, in0=dt, scalar=0.0, in1=t1, op0=ALU.max, op1=ALU.add
                                           ).then_inc(s["dt"], 1)
            dve.wait_ge(s["dt"], 1)
            dve.wait_ge(s["A_exp"], 1)
            nc.vector.tensor_scalar(t1, dt, col[0:H, SSDH + 2:SSDH + 3], -1.0, ALU.mult, ALU.mult).then_inc(s["dA"], 1)
            dve.wait_ge(s["dA"], 1)
            nc.vector.tensor_tensor_scan(cum, keep[0:H, :], t1, 0.0, ALU.mult, ALU.add).then_inc(s["cum"], 1)
            dve.wait_ge(s["cum"], 1)
            nc.vector.tensor_tensor(by_chunk(t1), by_chunk(cum)[:, :, C - 1:C].to_broadcast([H, NC, C]), by_chunk(cum),
                                    ALU.subtract).then_inc(s["c_end"], 1)
            dve.wait_ge(s["e_c_end"], 1)
            nc.vector.tensor_tensor(t1, t1, dt, ALU.mult).then_inc(s["dt_end"], 1)
            dve.wait_ge(s["eC"], 1)
            nc.vector.tensor_tensor(diag, by_chunk(eC)[:, :, C - 1:C].to_broadcast([H, NC, H]),
                                    m["ident"][0:H, 0:H].unsqueeze(1).to_broadcast([H, NC, H]),
                                    ALU.mult).then_inc(s["diag"], 1)
            dve.wait_ge(s["raw_zero"], 2)

            def tile(i, u):
                n = 2 * i + u
                out = xbc[:, bass.ds(n, 1), :].rearrange("p a t -> p (a t)")
                dve.wait_ge(s["raw"], n + 1)
                nc.vector.tensor_scalar(out, raw[u][:, 0:T], col[:, bass.ds(CONVW + n * TAPS, 1)],
                                        col[:, bass.ds(CONVB + n, 1)], ALU.mult, ALU.add).then_inc(s["conv"], 1)
                for j in range(1, TAPS):
                    dve.wait_ge(s["conv"], TAPS * n + j)
                    nc.vector.scalar_tensor_tensor(out=out, in0=raw[u][:, j:j + T],
                                                   scalar=col[:, bass.ds(CONVW + n * TAPS + j, 1)], in1=out,
                                                   op0=ALU.mult, op1=ALU.add).then_inc(s["conv"], 1)
                dve.wait_ge(s["xbc_sig"], n + 1)
                nc.vector.tensor_tensor(out, out, sig, ALU.mult).then_inc(s["xbc"], 1)
            tile(0, 0)
            tile(0, 1)
            with dve.Fori(1, CT // 2) as i:
                tile(i, 0)
                tile(i, 1)


def ssd(nc, m, s, io):
    H, SP = SSD_HEADS, SSD_P
    xbc = seg(m["D"], XBC, CT, T)
    sel = m["D"][0:H, SEL:SEL + H * P].rearrange("p (h x) -> p h x", h=H)
    ssn = seg(m["D"], SSN, 4 * NB, H)
    decay = seg(m["D"], DECAY, NC, H)
    cum = m["D"][0:H, CUM:CUM + T]
    z = seg(m["C"], 0, NB, D)
    mixed_t = seg(m["B"], 0, MT, T)
    xb = seg(m["A"], 0, CT, P)
    xs = seg(m["A"], 1536, H, SP)
    xdt = seg(m["A"], 2560, H, SP)
    xend = seg(m["A"], 3584, H, SP)
    L = seg(m["A"], 4608, H, P)
    b_nat = seg(m["A"], 6656, 2, P)
    cb = seg(m["A"], 6912, 2, P)
    state = seg(m["A"], 7168, H, SP)
    y = seg(m["D"], 16128, H, SP)
    y_flat = seg(m["D"], 16128, D)
    col, ps, ss = m["col"], m["ps"], m["ss"]

    def heads(lo):
        return ps[:, lo:lo + 2, :].rearrange("p u (h x) -> p (u h) x", x=SP)

    def of_block(b, q):
        return ssn[:, bass.ds(4 * b + q, 1), :].rearrange("p a h -> p (a h)")

    with nc.Block() as block:
        @block.sync
        def _(sp):
            sp.dma_start(m["D"][0:H, SEL:SEL + H * P], io["sel"]).then_inc(s["sel"], 16)

        @block.gpsimd
        def _(pool):
            def take(b):
                if not first(b):
                    pool.wait_ge(s["yoff_psum"], 2 * b)
                    pool.sem_inc(s["pool_gate"], 1)
                nc.gpsimd.tensor_copy(xb, xbc[:, :, bass.ds(b * P, P)]).then_inc(s["xb"], 1)
            take(0)
            with pool.Fori(1, NB) as b:
                take(b)

        @block.tensor
        def _(pe):
            pe.wait_ge(s["sel"], 16)

            def blk(b):
                pe.wait_ge(s["xb"], b + 1)
                if not first(b):
                    pe.wait_ge(s["y_mixed"], b)
                for c in range(8):
                    last = nc.tensor.transpose(ps[:, c // 4, (c % 4) * P:(c % 4 + 1) * P], xb[:, c, :], m["ident"][:])
                last.then_inc(s["xs_psum"], 1)
                for g in range(2):
                    nc.tensor.transpose(ps[:, 2, g * P:(g + 1) * P], xb[:, 8 + g, :], m["ident"][:])
                for g in range(2):
                    last = nc.tensor.matmul(ps[:, 2, (2 + g) * P:(3 + g) * P], xb[:, 8 + g, :], xb[:, 10 + g, :],
                                            start=True, stop=True)
                last.then_inc(s["b_psum"], 1)
                if not first(b):
                    pe.wait_ge(s["ssd_state"], 2 * b + 1)
                    pe.wait_ge(s["y_off"], b)
                for h in range(H):
                    last = nc.tensor.matmul(ps[:, 3 + h // 4, (h % 4) * P:(h % 4 + 1) * P], sel[:, h, :],
                                            cum[:, bass.ds(b * P, P)], start=True, stop=True)
                last.then_inc(s["row_psum"], 1)
                pe.wait_ge(s["diff"], 2 * b + 1)
                for c in range(2):
                    pe.wait_ge(s["ssd_state"], 2 * b + c + 1)
                    for g in range(2):
                        last = nc.tensor.matmul(ps[c * C:(c + 1) * C, 3 + g, :], xb[:, 10 + g, c * C:(c + 1) * C],
                                                state[:, g * 8:(g + 1) * 8, :], start=True, stop=True)
                    last.then_inc(s["yoff_psum"], 1)
                    if c == 0:
                        pe.wait_ge(s["b_nat"], b + 1)
                        pe.wait_ge(s["xend"], b + 1)
                    for g in range(2):
                        last = nc.tensor.matmul(ps[:, 5 + g, :], b_nat[c * C:(c + 1) * C, g, :],
                                                xend[c * C:(c + 1) * C, g * 8:(g + 1) * 8, :], start=True, stop=True)
                    last.then_inc(s["sum_psum"], 1)
                pe.wait_ge(s["weights"], b + 1)
                pe.wait_ge(s["xdt"], b + 1)
                pe.wait_ge(s["xs"], b + 1)
                for h in range(H):
                    last = nc.tensor.matmul(ps[:, h // 8, (h % 8) * SP:(h % 8 + 1) * SP], L[:, h, :], xdt[:, h, :],
                                            start=True, stop=True)
                last.then_inc(s["ydiag_psum"], 1)
                pe.wait_ge(s["y_normed"], 2 * b + 2)
                for c in range(8):
                    last = nc.tensor.transpose(ps[:, c // 4, (c % 4) * P:(c % 4 + 1) * P],
                                               y_flat[:, c * P:(c + 1) * P], m["ident"][:])
                last.then_inc(s["yT_psum"], 1)
            blk(0)
            with pe.Fori(1, NB) as b:
                blk(b)

        @block.scalar
        def _(act):
            def blk(b):
                act.wait_ge(s["xs_psum"], b + 1)
                if not first(b):
                    act.wait_ge(s["y_skip"], b)
                nc.scalar.copy(xs, heads(0)).then_inc(s["xs"], 1)
                act.wait_ge(s["b_psum"], b + 1)
                if not first(b):
                    act.wait_ge(s["sum_psum"], 2 * b)
                nc.scalar.copy(b_nat, ps[:, 2, 0:2 * P].rearrange("p (g x) -> p g x", g=2)).then_inc(s["b_nat"], 1)
                act.wait_ge(s["diff"], 2 * b + 2)
                nc.scalar.activation(L, L, ACT.Exp).then_inc(s["L"], 1)
                act.wait_ge(s["y_gated"], b + 1)
                for g in range(2):
                    nc.scalar.activation(L[:, g * 4:(g + 1) * 4, :].rearrange("p a b -> p (a b)"),
                                         y_flat[:, g * 512:(g + 1) * 512], ACT.Square,
                                         accum_out=ss[:, g:g + 1]).then_inc(s["y_squared"], 1)
                act.wait_ge(s["y_mean"], b + 1)
                nc.scalar.activation(ss[:, 2:4], ss[:, 2:4], ACT.Sqrt).then_inc(s["y_root"], 1)
                act.wait_ge(s["y_rstd"], b + 1)
                for g in range(2):
                    part = y_flat[:, g * 512:(g + 1) * 512]
                    nc.scalar.activation(part, part, ACT.Copy, scale=ss[:, 4 + g:5 + g]).then_inc(s["y_normed"], 1)
            blk(0)
            with act.Fori(1, NB) as b:
                blk(b)

        @block.vector
        def _(dve):
            nc.vector.memset(cb, 0.0).then_inc(s["cb_zero"], 1)
            nc.vector.memset(state, 0.0).then_inc(s["ssd_state"], 1)
            dve.wait_ge(s["cb_zero"], 1)

            def blk(b):
                def over_channels(q):
                    return of_block(b, q).unsqueeze(2).to_broadcast([P, H, SP])
                dve.wait_ge(s["xs"], b + 1)
                if not first(b):
                    dve.wait_ge(s["ydiag_psum"], b)
                nc.vector.tensor_tensor(xdt, xs, over_channels(0), ALU.mult).then_inc(s["xdt"], 1)
                nc.vector.tensor_tensor(xend, xs, over_channels(3), ALU.mult).then_inc(s["xend"], 1)
                dve.wait_ge(s["row_psum"], b + 1)
                nc.vector.tensor_tensor(L, ps[:, 3:7, :].rearrange("p u (h x) -> p (u h) x", x=P),
                                        of_block(b, 1).unsqueeze(2).to_broadcast([P, H, P]),
                                        ALU.subtract).then_inc(s["diff"], 1)
                dve.wait_ge(s["diff"], 2 * b + 1)
                nc.vector.tensor_scalar(L, L, 0.0, None, ALU.min).then_inc(s["diff"], 1)
                nc.vector.tensor_tensor(xs, xs, col[:, DROW:DROW + H].unsqueeze(2).to_broadcast([P, H, SP]),
                                        ALU.mult).then_inc(s["x_skip"], 1)
                dve.wait_ge(s["b_psum"], b + 1)
                dve.wait_ge(s["b_nat"], b + 1)
                if not first(b):
                    dve.wait_ge(s["weights"], b)
                dve.sem_inc(s["dve_gate"], 1)
                for g in range(2):
                    nc.vector.copy_predicated(cb[:, g, :], m["mask"][:], ps[:, 2, (2 + g) * P:(3 + g) * P]
                                              ).then_inc(s["cb"], 1)
                for c in range(2):
                    dve.wait_ge(s["yoff_psum"], 2 * b + c + 1)
                    dve.wait_ge(s["ssd_state"], 2 * b + c + 1)
                    nc.vector.tensor_tensor(state, state, decay[:, bass.ds(2 * b + c, 1), :].rearrange("p a h -> p (a h)")
                                            .unsqueeze(2).to_broadcast([P, H, SP]), ALU.mult).then_inc(s["decayed"], 1)
                    dve.wait_ge(s["decayed"], 2 * b + c + 1)
                    dve.wait_ge(s["sum_psum"], 2 * b + c + 1)
                    nc.vector.tensor_tensor(state, state, heads(5), ALU.add).then_inc(s["ssd_state"], 1)
                    if c == 0:
                        dve.wait_ge(s["L"], b + 1)
                        dve.wait_ge(s["cb"], 2 * b + 2)
                        for g in range(2):
                            part = L[:, g * 8:(g + 1) * 8, :]
                            last = nc.vector.tensor_tensor(part, part, cb[:, g:g + 1, :].to_broadcast([P, 8, P]), ALU.mult)
                        last.then_inc(s["weights"], 1)
                if not first(b):
                    dve.wait_ge(s["yT_psum"], b)
                nc.vector.tensor_tensor(y, heads(3), over_channels(2), ALU.mult).then_inc(s["y_off"], 1)
                dve.wait_ge(s["y_off"], b + 1)
                dve.wait_ge(s["ydiag_psum"], b + 1)
                nc.vector.tensor_tensor(y, y, heads(0), ALU.add).then_inc(s["y_sum"], 1)
                dve.wait_ge(s["y_sum"], b + 1)
                dve.wait_ge(s["x_skip"], b + 1)
                nc.vector.tensor_tensor(y, y, xs, ALU.add).then_inc(s["y_skip"], 1)
                dve.wait_ge(s["y_skip"], b + 1)
                nc.vector.tensor_tensor(y_flat, y_flat, z[:, bass.ds(b, 1), :].rearrange("p a d -> p (a d)"),
                                        ALU.mult).then_inc(s["y_gated"], 1)
                dve.wait_ge(s["y_squared"], 2 * b + 2)
                nc.vector.tensor_scalar(ss[:, 2:4], ss[:, 0:2], 1.0 / 512, EPS, ALU.mult, ALU.add).then_inc(s["y_mean"], 1)
                dve.wait_ge(s["y_root"], b + 1)
                nc.vector.reciprocal(ss[:, 4:6], ss[:, 2:4]).then_inc(s["y_rstd"], 1)
                dve.wait_ge(s["yT_psum"], b + 1)
                nc.vector.tensor_tensor(mixed_t[:, 8:16, bass.ds(b * P, P)],
                                        ps[:, 0:2, :].rearrange("p u (c t) -> p (u c) t", c=4),
                                        col[:, SSDW:SSDW + 8].unsqueeze(2).to_broadcast([P, 8, P]),
                                        ALU.mult).then_inc(s["y_mixed"], 1)
            blk(0)
            with dve.Fori(1, NB) as b:
                blk(b)


def project_out(nc, m, s, io):
    mixed_t = seg(m["B"], 0, MT, T)
    x2 = seg(m["A"], 0, NB, D)
    with nc.Block() as block:
        @block.sync
        def _(sp):
            for c in range(2):
                sp.dma_start(seg(m["D"], 8192 * c, 8192), io["w_out"][c]).then_inc(s[f"half_w{c}"], 16)
                if c == 0:
                    sp.dma_start(x2, io["x"].rearrange("(b p) d -> p b d", p=P)).then_inc(s["x_again"], 16)
                    sp.dma_start(m["nrow"][:], io["norm_ffn_row"]).then_inc(s["ffn_row"], 16)

        @block.tensor
        def _(pe):
            natural_groups(nc, pe, m, s, mixed_t, [seg(m["D"], 8192 * c, 8192) for c in range(2)], MT,
                           2, "x2", 8)

        @block.vector
        def _(dve):
            dve.wait_ge(s["x_again"], 16)
            for n in range(16):
                part = x2[:, n % NB, (n // NB) * 512:(n // NB + 1) * 512]
                dve.wait_ge(s["half_psum"], 32 + n + 1)
                nc.vector.tensor_tensor(part, part, m["ps"][:, n % 8, :], ALU.add).then_inc(s["x2"], 1)


WQ, QT, KEYS = 8192, 10240, 12288
SC, CAND, ONEHOT = 12544, 13056, 13312
TOPV, TOPF, BESTV, GATE = 13824, 13856, 13888, 14016
ACTV, IDS, DIAG = 14144, 14208, 14336


def norm_ffn(nc, m, s, io):
    with nc.Block() as block:
        @block.sync
        def _(sp):
            sp.dma_start(seg(m["B"], WQ, 2048), io["w_query"][0]).then_inc(s["wq"], 16)
            sp.dma_start(seg(m["B"], KEYS, 256), io["keys"][0]).then_inc(s["keys"], 16)
        norm_blocks(nc, block, m, s, NB, seg(m["A"], 0, NB, D), seg(m["C"], 0, NB, D), seg(m["B"], 0, KT, T),
                    m["D"][:, 0:D], (s["ffn_row"], 16))


def peer(nc, m, s, io):
    x2 = seg(m["A"], 0, NB, D)
    h2 = seg(m["C"], 0, NB, D)
    h2_t = seg(m["B"], 0, KT, T)
    ring = seg(m["D"], 0, RING, 2 * D)
    wq = seg(m["B"], WQ, 2, KT, P)
    q_t = seg(m["B"], QT, 2, T)
    keys = seg(m["B"], KEYS, 2, NK)
    sc = seg(m["B"], SC, 2, 2, NK)
    cand = seg(m["B"], CAND, K, K)
    cand_flat = seg(m["B"], CAND, K * K)
    onehot = seg(m["B"], ONEHOT, 2 * K, K)
    top_v = seg(m["B"], TOPV, 2, K)
    top_f = seg(m["B"], TOPF, 2, K)
    best_v = seg(m["B"], BESTV, NB, K)
    gate = seg(m["B"], GATE, NB, K)
    a_raw, a_gelu, a_gated, picked = (seg(m["B"], ACTV + 16 * i, K) for i in range(4))
    place_f = seg(m["B"], IDS, 2, K)
    picked_ids = seg(m["B"], IDS + 32, 2, K)
    gate_sum = seg(m["B"], IDS + 64, NB)
    gate_rec = seg(m["B"], IDS + 72, NB)
    ps, col = m["ps"], m["col"]
    top_i, best_i, place, ids = (handle[:] for handle in m["u32"])
    diag = seg(m["B"], DIAG, 2 * PAIR, P)
    GROUPS = K // PAIR
    HALF_K, HALF_RING = K // 2, RING // 2
    STEPS = 25

    with nc.Block() as block:
        @block.sync
        def _(sp):
            with sp.Fori(0, PH - 1) as hd:
                sp.wait_ge(s["q_psum2"], 2 * (hd + 1))
                sp.dma_start(seg(m["B"], WQ, 2048), io["w_query"][bass.ds(hd + 1, 1)].rearrange("a p n -> p (a n)")
                             ).then_inc(s["wq"], 16)
                sp.wait_ge(s["sc_psum"], NB * (hd + 1))
                sp.dma_start(seg(m["B"], KEYS, 256), io["keys"][bass.ds(hd + 1, 1)].rearrange("a p n -> p (a n)")
                             ).then_inc(s["keys"], 16)

        @block.tensor
        def _(pe):
            def project(hd):
                pe.wait_ge(s["wq"], 16 * (hd + 1))
                if not first(hd):
                    pe.wait_ge(s["q_t"], 2 * hd)
                for half in range(2):
                    for u in range(2):
                        for kt in range(KT):
                            last = nc.tensor.matmul(ps[:, 2 * half + u, :], wq[:, half, kt, :],
                                                    h2_t[:, kt, u * 512:(u + 1) * 512], start=(kt == 0), stop=(kt == KT - 1))
                    last.then_inc(s["q_psum2"], 1)

            def project_step(hd, b, i):
                half, u, kt = b // 4, b // 2 % 2, b % 2 * 4 + i
                if b == 0 and i == 0:
                    pe.wait_ge(s["wq"], 16 * (hd + 1))
                last = nc.tensor.matmul(ps[:, 2 * half + u, :], wq[:, half, kt, :],
                                        h2_t[:, kt, u * 512:(u + 1) * 512], start=(kt == 0), stop=(kt == KT - 1))
                if b % 4 == 3 and i == 3:
                    last.then_inc(s["q_psum2"], 1)

            def score(hd, b):
                if b == 0:
                    pe.wait_ge(s["q_t"], 2 * (hd + 1))
                    pe.wait_ge(s["keys"], 16 * (hd + 1))
                if not (first(hd) and b < 2):
                    pe.wait_ge(s["sc"], NB * hd + b - 1)
                for half in range(2):
                    last = nc.tensor.matmul(ps[:, 4 + b % 2, half * NK:(half + 1) * NK],
                                            q_t[:, half, b * P:(b + 1) * P], keys[:, half, :], start=True, stop=True)
                last.then_inc(s["sc_psum"], 1)

            def body(hd, prepare, ahead):
                for b in range(NB):
                    it = NB * hd + b
                    if prepare and b == 0:
                        score(hd + 1, 0)
                    for q in range(GROUPS // 2):
                        if q == 0:
                            pe.wait_ge(s["expert_banks"], it + 1)
                        for i in range(PAIR):
                            n = PAIR * q + i
                            slot = PAIR * (2 * q + 1) + i
                            pe.wait_ge(s["diag_done"], it * HALF_K + n + 1)
                            for u in range(2):
                                last = nc.tensor.matmul(
                                    ps[:, 6 + u, :], diag[:, n % (2 * PAIR), :],
                                    ring[:, slot % RING, D + u * 512:D + (u + 1) * 512],
                                    start=(n == 0), stop=(n == HALF_K - 1), skip_group_check=True)
                            last.then_inc(s["slot_free_pe"], 1)
                        if ahead:
                            project_step(hd + 2, b, q)
                        if prepare and q == 1 and b + 1 < NB:
                            score(hd + 1, b + 1)
            project(0)
            for b in range(NB):
                score(0, b)
            project(1)
            with pe.Fori(0, PH - 2) as hd:
                body(hd, True, True)
            body(PH - 2, True, False)
            body(PH - 1, False, False)

        @block.gpsimd
        def _(pool):
            def item(hd, b):
                pool.wait_ge(s["ids"], NB * hd + b + 1)
                pool.sem_inc(s["pool_gate"], 1)
                for j in range(K):
                    r = j % RING
                    owner, n = ("slot_free_pe" if j // PAIR % 2 else "slot_free"), j // (2 * PAIR) * PAIR + j % PAIR
                    pool.wait_ge(s[owner], (NB * hd + b) * HALF_K + n + 1)
                    pool.sem_inc(s["pool_gate"], 1)
                    pool.indirect_dma_start(ring[:, r, :], None, io["experts"],
                                            bass.IndirectOffsetOnAxis(ap=ids[:, b, j:j + 1], axis=0)
                                            ).then_inc(s[f"rows{r}"], 16)
            with pool.Fori(0, PH) as hd:
                for b in range(NB):
                    item(hd, b)

        @block.scalar
        def _(act):
            def take_queries(hd):
                for half in range(2):
                    act.wait_ge(s["q_psum2"], 2 * hd + half + 1)
                    if half == 0 and not first(hd):
                        act.wait_ge(s["sc_psum"], NB * hd)
                    nc.scalar.copy(q_t[:, half, :], ps[:, 2 * half:2 * half + 2, :].rearrange("p a b -> p (a b)")
                                   ).then_inc(s["q_t"], 1)

            def take_scores(hd, b):
                act.wait_ge(s["sc_psum"], NB * hd + b + 1)
                if not (first(hd) and b < 2):
                    act.wait_ge(s["ids"], NB * hd + b - 1)
                nc.scalar.copy(sc[:, b % 2, :, :], ps[:, 4 + b % 2, 0:2 * NK].rearrange("p (a k) -> p a k", a=2)
                               ).then_inc(s["sc"], 1)

            def diagonals(hd, b, g):
                it = NB * hd + b
                act.wait_ge(s["gated"], it * GROUPS + g + 1)
                for i in range(PAIR):
                    n = g // 2 * PAIR + i
                    act.wait_ge(s["slot_free_pe"], it * HALF_K + n + 1)
                    nc.scalar.activation(diag[:, n % (2 * PAIR), :], m["ident"][:], ACT.Copy,
                                         scale=a_gated[:, PAIR * g + i:PAIR * g + i + 1]).then_inc(s["diag_done"], 1)

            def gate_exp(hd):
                act.wait_ge(s["gate_diff"], hd + 1)
                nc.scalar.activation(gate, gate, ACT.Exp).then_inc(s["gate_exp"], 1)

            def body(hd, prepare):
                for b in range(NB):
                    if b == 0 and prepare:
                        take_queries(hd + 1)
                        take_scores(hd + 1, 0)
                    for g in range(GROUPS):
                        act.wait_ge(s["dots"], (NB * hd + b) * K + PAIR * (g + 1))
                        nc.scalar.activation(a_gelu[:, PAIR * g:PAIR * (g + 1)], a_raw[:, PAIR * g:PAIR * (g + 1)],
                                             ACT.Gelu).then_inc(s["gelu"], 1)
                        if g % 2 == 1:
                            diagonals(hd, b, g)
                        if g == 6 and prepare and b + 1 < NB:
                            take_scores(hd + 1, b + 1)
                if prepare:
                    gate_exp(hd + 1)
            take_queries(0)
            for b in range(NB):
                take_scores(0, b)
            gate_exp(0)
            with act.Fori(0, PH - 1) as hd:
                body(hd, True)
            body(PH - 1, False)

        @block.vector
        def _(dve):
            dve.sem_inc(s["slot_free"], HALF_RING)
            dve.sem_inc(s["slot_free_pe"], HALF_RING)
            dve.sem_inc(s["expert_banks"], 1)

            def pick(hd, b):
                done = [0]

                def step(ins):
                    ins.then_inc(s["pick"], 1)
                    done[0] += 1

                def former_steps():
                    dve.wait_ge(s["pick"], (NB * hd + b) * STEPS + done[0])
                    dve.sem_inc(s["dve_gate"], 1)
                half_sc = [sc[:, b % 2, half, :] for half in range(2)]
                dve.wait_ge(s["sc"], NB * hd + b + 1)
                dve.sem_inc(s["dve_gate"], 1)
                for rank in (0, 8):
                    for half in range(2):
                        step(nc.vector.max(top_v[:, half, rank:rank + 8], half_sc[half]))
                    yield
                    former_steps()
                    for half in range(2):
                        step(nc.vector.max_index(top_i[:, half, rank:rank + 8], top_v[:, half, rank:rank + 8], half_sc[half]))
                    if rank == 0:
                        for half in range(2):
                            step(nc.vector.match_replace(half_sc[half], top_v[:, half, 0:8], half_sc[half], LOWEST))
                    yield
                    former_steps()
                step(nc.vector.tensor_copy(top_f, top_i))
                step(nc.vector.tensor_tensor(cand, top_v[:, 0, :].unsqueeze(2).to_broadcast([P, K, K]),
                                             top_v[:, 1:2, :].to_broadcast([P, K, K]), ALU.add))
                yield
                former_steps()
                for rank in (0, 8):
                    step(nc.vector.max(best_v[:, b, rank:rank + 8], cand_flat))
                    yield
                    former_steps()
                    step(nc.vector.max_index(best_i[:, rank:rank + 8], best_v[:, b, rank:rank + 8], cand_flat))
                    if rank == 0:
                        step(nc.vector.match_replace(cand_flat, best_v[:, b, 0:8], cand_flat, LOWEST))
                    yield
                    former_steps()
                step(nc.vector.tensor_scalar(place[:, 0, :], best_i, 4, None, ALU.logical_shift_right))
                step(nc.vector.tensor_scalar(place[:, 1, :], best_i, 15, None, ALU.bitwise_and))
                yield
                former_steps()
                step(nc.vector.tensor_copy(place_f, place))
                yield
                former_steps()
                step(nc.vector.tensor_tensor(
                    onehot, place_f.rearrange("p a j -> p (a j)").unsqueeze(2).to_broadcast([P, 2 * K, K]),
                    col[:, IOTA:IOTA + K].unsqueeze(1).to_broadcast([P, 2 * K, K]), ALU.is_equal))
                yield
                former_steps()
                for half in range(2):
                    part = onehot[:, half * K:(half + 1) * K, :]
                    step(nc.vector.tensor_tensor(part, part, top_f[:, half:half + 1, :].to_broadcast([P, K, K]), ALU.mult))
                yield
                former_steps()
                step(nc.vector.tensor_reduce(picked_ids.rearrange("p a j -> p (a j)"), onehot, AX_X, ALU.add))
                yield
                former_steps()
                step(nc.vector.tensor_scalar(picked, picked_ids[:, 0, :], float(NK), None, ALU.mult))
                yield
                former_steps()
                nc.vector.tensor_tensor(ids[:, b, :], picked, picked_ids[:, 1, :], ALU.add).then_inc(s["ids"], 1)
                assert done[0] == STEPS

            def gates(hd):
                dve.wait_ge(s["ids"], NB * (hd + 1))
                nc.vector.tensor_tensor(gate, best_v, best_v[:, :, 0:1].to_broadcast([P, NB, K]), ALU.subtract
                                        ).then_inc(s["gate_diff"], 1)
                dve.wait_ge(s["gate_exp"], hd + 1)
                nc.vector.tensor_reduce(gate_sum, gate, AX_X, ALU.add).then_inc(s["gate_sum"], 1)
                dve.wait_ge(s["gate_sum"], hd + 1)
                nc.vector.reciprocal(gate_rec, gate_sum).then_inc(s["gate_rec"], 1)
                dve.wait_ge(s["gate_rec"], hd + 1)
                nc.vector.tensor_tensor(gate, gate, gate_rec.unsqueeze(2).to_broadcast([P, NB, K]), ALU.mult
                                        ).then_inc(s["gates"], 1)

            def dots(hd, b, g):
                for j in range(PAIR * g, PAIR * (g + 1)):
                    use = (NB * hd + b) * (K // RING) + j // RING
                    dve.wait_ge(s[f"rows{j % RING}"], 16 * (use + 1))
                    u_rows = ring[:, j % RING, 0:D]
                    nc.vector.tensor_tensor_reduce(u_rows, u_rows, h2[:, b, :], 1.0, 0.0, ALU.mult, ALU.add,
                                                   a_raw[:, j:j + 1]).then_inc(s["dots"], 1)

            def add_experts(hd, b, g):
                it = NB * hd + b
                cols = slice(PAIR * g, PAIR * (g + 1))
                dve.wait_ge(s["gelu"], it * GROUPS + g + 1)
                nc.vector.tensor_tensor(a_gated[:, cols], a_gelu[:, cols], gate[:, b, cols], ALU.mult
                                        ).then_inc(s["gated"], 1)
                if g % 2 == 1:
                    return
                dve.wait_ge(s["gated"], it * GROUPS + g + 1)
                for j in range(PAIR * g, PAIR * (g + 1)):
                    n = g // 2 * PAIR + j % PAIR
                    dve.wait_ge(s["slot_free"], it * HALF_K + n + HALF_RING)
                    nc.vector.scalar_tensor_tensor(out=x2[:, b, :], in0=ring[:, j % RING, D:2 * D],
                                                   scalar=a_gated[:, j:j + 1], in1=x2[:, b, :],
                                                   op0=ALU.mult, op1=ALU.add).then_inc(s["slot_free"], 1)

            def add_bank_sums(hd, b):
                it = NB * hd + b
                dve.wait_ge(s["slot_free_pe"], it * HALF_K + HALF_K + HALF_RING)
                dve.wait_ge(s["slot_free"], it * HALF_K + HALF_K + HALF_RING)
                nc.vector.tensor_tensor(x2[:, b, :], x2[:, b, :], ps[:, 6:8, :].rearrange("p u n -> p (u n)"), ALU.add
                                        ).then_inc(s["expert_banks"], 1)

            def body(hd, prepare):
                dve.wait_ge(s["gates"], hd + 1)
                for b in range(NB):
                    dve.wait_ge(s["expert_banks"], NB * hd + b + 1)
                    picking = pick(hd + 1, b) if prepare else iter(())
                    for g in range(GROUPS):
                        dots(hd, b, g)
                        next(picking, None)
                        next(picking, None)
                        add_experts(hd, b, g)
                    for _ in picking:
                        pass
                    add_bank_sums(hd, b)
                if prepare:
                    gates(hd + 1)
            for b in range(NB):
                for _ in pick(0, b):
                    pass
            gates(0)
            with dve.Fori(0, PH - 1) as hd:
                body(hd, True)
            body(PH - 1, False)


def norm_final(nc, m, s, io):
    x2 = seg(m["A"], 0, NB, D)
    out = seg(m["C"], 0, NB, D)
    ss = m["ss"]
    with nc.Block() as block:
        @block.sync
        def _(sp):
            sp.dma_start(m["nrow"][:], io["final_row"]).then_inc(s["final_row"], 16)
            for b in range(NB):
                sp.wait_ge(s["final"], b + 1)
                sp.dma_start(io["out"][b * P:(b + 1) * P, :], out[:, b, :]).then_inc(s["written"], 16)
            sp.wait_ge(s["written"], 16 * NB)

        @block.scalar
        def _(act):
            for b in range(NB):
                nc.scalar.activation(out[:, b, :], x2[:, b, :], ACT.Square, accum_out=ss[:, b:b + 1]
                                     ).then_inc(s["squared"], 1)
            act.wait_ge(s["mean"], 3)
            nc.scalar.activation(ss[:, 8:16], ss[:, 8:16], ACT.Sqrt).then_inc(s["root"], 1)

        @block.vector
        def _(dve):
            dve.wait_ge(s["final_row"], 16)
            dve.wait_ge(s["squared"], 3 * NB)
            nc.vector.tensor_scalar(ss[:, 8:16], ss[:, 0:8], 1.0 / D, EPS, ALU.mult, ALU.add).then_inc(s["mean"], 1)
            dve.wait_ge(s["root"], 3)
            nc.vector.reciprocal(ss[:, 16:24], ss[:, 8:16]).then_inc(s["rstd"], 1)
            dve.wait_ge(s["rstd"], 3)
            for b in range(NB):
                nc.vector.scalar_tensor_tensor(out=out[:, b, :], in0=x2[:, b, :], scalar=ss[:, 16 + b:17 + b],
                                               in1=m["nrow"][:], op0=ALU.mult, op1=ALU.mult).then_inc(s["final"], 1)


def kernel(**inputs):
    import numpy as np
    import concourse.bacc as bacc
    from concourse.bass_utils import run_bass_kernel_spmd

    a = {n: np.asarray(v) for n, v in inputs.items()}
    w_in = a["w_in"][0]
    W = D

    def tiles(w, n):
        return np.ascontiguousarray(w.reshape(w.shape[0] // P, P, n, -1).transpose(2, 1, 0, 3).reshape(n, P, -1))

    def rows(v):
        return np.ascontiguousarray(np.broadcast_to(v.reshape(1, -1), (P, v.size)))

    def columns(v):
        return v.reshape(-1, P).T

    cols = np.zeros((P, TMP), np.float32)
    cols[:, LBL:LBL + 8] = columns(a["hg_lb_logits"][0])
    cols[:, LBL + 8:LBL + 16] = columns(a["hg_lb_logits"][1])
    cols[:, HGW:HGW + 1] = columns(a["hg_norm_w"][0])
    cols[:, CONVW:CONVW + CT * TAPS] = a["ssd_conv_w"][0].reshape(TAPS, CT, P).transpose(2, 1, 0).reshape(P, CT * TAPS)
    cols[:, CONVB:CONVB + CT] = columns(a["ssd_conv_b"][0])
    cols[:, SSDW:SSDW + 8] = columns(a["ssd_norm_w"][0])
    cols[0:SSD_HEADS, SSDH] = a["ssd_dt_bias"][0]
    cols[0:SSD_HEADS, SSDH + 1] = a["ssd_A_log"][0]
    cols[:, DROW:DROW + SSD_HEADS] = rows(a["ssd_D"][0])
    cols[:, IOTA:IOTA + K] = np.arange(K)
    t = np.arange(P)
    sel = np.zeros((SSD_HEADS, SSD_HEADS, P), np.float32)
    sel[np.arange(SSD_HEADS), np.arange(SSD_HEADS)] = 1
    keep = np.ones((P, T), np.float32)
    keep[:, ::C] = 0
    arrays = {
        "x": np.ascontiguousarray(a["x"][0]),
        "norm_mix_row": rows(a["norm_mix_w"][0]),
        "norm_ffn_row": rows(a["norm_ffn_w"][0]),
        "final_row": rows(a["final_norm_w"]),
        "cols": cols,
        "ident": np.eye(P, dtype=np.float32),
        "mask": ((t[:, None] <= t[None, :]) & (t[:, None] // C == t[None, :] // C)).astype(np.uint32),
        "keep": keep,
        "sel": sel.reshape(SSD_HEADS, -1),
        "w_v": tiles(w_in[:, 2 * W:3 * W], 2),
        "w_hg": np.ascontiguousarray(np.concatenate([tiles(w_in[:, W:2 * W], 8), tiles(w_in[:, 3 * W:4 * W], 8),
                                                     tiles(w_in[:, 0:W], 8)], axis=2)),
        "w_z": tiles(w_in[:, 4 * W:5 * W], 2),
        "w_xbc": tiles(w_in[:, 5 * W:5 * W + CT * P], CT),
        "w_dt": tiles(w_in[:, 5 * W + CT * P:], 1)[0],
        "w_out": tiles(a["w_out"][0], 2),
        "w_query": np.ascontiguousarray(tiles(a["peer_w_q"][0], 16).reshape(PH, 2, P, D).transpose(0, 2, 1, 3).reshape(PH, P, 2 * D)),
        "keys": np.ascontiguousarray(a["peer_keys"][0].transpose(0, 3, 1, 2).reshape(PH, P, 2 * NK)),
        "experts": np.concatenate([a["peer_u"][0], a["peer_v"][0]], axis=1),
    }
    nc = bacc.Bacc("TRN2", target_bir_lowering=False, num_devices=1)
    io = {n: nc.dram_tensor("in_" + n, v.shape, mybir.dt.from_np(v.dtype), kind="ExternalInput").ap()
          for n, v in arrays.items()}
    out = nc.dram_tensor("out_x", (1, T, D), F32, kind="ExternalOutput").ap()
    io["out"] = out.rearrange("a t d -> (a t) d")
    layer(nc, io)
    r = run_bass_kernel_spmd(nc, [{"in_" + n: v for n, v in arrays.items()}], core_ids=[0])
    return r.results[0]["out_x"]
```

```python
import itertools
from contextlib import ExitStack

import concourse.bass as bass
from concourse import mybir

F32 = mybir.dt.float32
U32 = mybir.dt.uint32
ALU = mybir.AluOpType
ACT = mybir.ActivationFunctionType
AX_X = mybir.AxisListType.X

P = 128
T = 1024
NB = T // P
D = 1024
KT = D // P
C = 64
NC = T // C
HG_HEADS = 8
SSD_HEADS = 16
SSD_P = 64
CT = 12
MT = 16
TAPS = 4
PH = 8
K = 16
NK = 128
EPS = 1e-6
LOWEST = -3.0e38
RING = 8
PAIR = 2


class Sems(dict):

    def __init__(self, ctx, nc):
        self.ctx, self.nc = ctx, nc

    def __missing__(self, name):
        self[name] = self.ctx.enter_context(self.nc.semaphore(name))
        return self[name]


def seg(region, start, *shape):
    size = 1
    for n in shape:
        size *= n
    ap = region[:, start:start + size]
    if len(shape) == 2:
        ap = ap.rearrange("p (a b) -> p a b", a=shape[0])
    elif len(shape) == 3:
        ap = ap.rearrange("p (a b c) -> p a b c", a=shape[0], b=shape[1])
    return ap


def first(n):
    return isinstance(n, int) and n == 0


def layer(nc, io):
    with ExitStack() as ctx:
        def sb(name, shape, dt=F32):
            return ctx.enter_context(nc.sbuf_tensor(name, shape, dt))

        m = {
            "A": sb("region_a", [P, 8192]),
            "B": sb("region_b", [P, 16384]),
            "C": sb("region_c", [P, 8192]),
            "D": sb("region_d", [P, 17408]),
            "ps": ctx.enter_context(nc.psum_tensor("ps", [P, 8, 512], F32)),
            "ident": sb("ident", [P, P]),
            "mask": sb("mask", [P, P], U32),
            "keep": sb("keep", [P, T]),
            "nrow": sb("nrow", [P, D]),
            "col": sb("col", [P, 160]),
            "ss": sb("ss", [P, 32]),
            "u32": (sb("top_i", [P, 2, K], U32), sb("best_i", [P, K], U32), sb("place", [P, 2, K], U32),
                    sb("ids", [P, NB, K], U32)),
        }
        s = Sems(ctx, nc)
        norm_in_and_v(nc, m, s, io)
        hgrn(nc, m, s, io)
        project_z(nc, m, s, io)
        project_xbc(nc, m, s, io)
        ssd(nc, m, s, io)
        project_out(nc, m, s, io)
        peer(nc, m, s, io)
        norm_final(nc, m, s, io)


LBL = 0
LB = 16
OMLB = 24
HGW = 32
CONVW = 33
CONVB = 81
SSDW = 93
SSDH = 101
DROW = 104
IOTA = 120
TMP = 136


def norm_blocks(nc, m, s, before, src, dst, dst_t, junk, ready):
    ps, ss = m["ps"], m["ss"]
    sq, mean, root, rstd, normed, turned, stored = (s[n] for n in (
        "squared", "mean", "root", "rstd", "normed", "turned", "stored"))
    HB = NB // 2

    def act_squares(act):
        for u in range(2):
            act.wait_ge(*ready[u])
            for b in range(HB * u, HB * (u + 1)):
                if b >= 1:
                    act.wait_ge(sq, before + b)
                nc.scalar.activation(junk, src[:, b, :], ACT.Square, accum_out=ss[:, b:b + 1]).then_inc(sq, 1)
            act.wait_ge(mean, before // HB + u + 1)
            half = ss[:, 8 + HB * u:8 + HB * (u + 1)]
            nc.scalar.activation(half, half, ACT.Sqrt).then_inc(root, 1)

    def act_store(act, b):
        act.wait_ge(turned, before + b + 1)
        nc.scalar.copy(dst_t[:, :, b * P:(b + 1) * P],
                       ps[:, 2 * (b % 2):2 * (b % 2) + 2, :].rearrange("p u (k t) -> p (u k) t", k=4)
                       ).then_inc(stored, 1)

    def dve_norm(dve):
        for u in range(2):
            count = before // HB + u + 1
            lo, hi = HB * u, HB * (u + 1)
            dve.wait_ge(*ready[u])
            dve.wait_ge(sq, before + hi)
            nc.vector.tensor_scalar(ss[:, 8 + lo:8 + hi], ss[:, lo:hi], 1.0 / D, EPS, ALU.mult, ALU.add
                                    ).then_inc(mean, 1)
            dve.wait_ge(root, count)
            nc.vector.reciprocal(ss[:, 16 + lo:16 + hi], ss[:, 8 + lo:8 + hi]).then_inc(rstd, 1)
            dve.wait_ge(rstd, count)
            for b in range(lo, hi):
                nc.vector.scalar_tensor_tensor(out=dst[:, b, :], in0=src[:, b, :], scalar=ss[:, 16 + b:17 + b],
                                               in1=m["nrow"][:], op0=ALU.mult, op1=ALU.mult).then_inc(normed, 1)

    def pe_turn(pe, b):
        pe.wait_ge(normed, before + b + 1)
        if b >= 2:
            pe.wait_ge(stored, before + b - 1)
        for k in range(KT):
            last = nc.tensor.transpose(ps[:, 2 * (b % 2) + k // 4, (k % 4) * P:(k % 4 + 1) * P],
                                       dst[:, b, k * P:(k + 1) * P], m["ident"][:])
        last.then_inc(turned, 1)

    return act_squares, act_store, dve_norm, pe_turn


def norm_in_and_v(nc, m, s, io):
    x_all = seg(m["C"], 0, NB, D)
    h_t = seg(m["A"], 0, KT, T)
    v = x_all
    w_v = [seg(m["D"], 4096 * c, 4096) for c in range(2)]
    col, ps = m["col"], m["ps"]
    act_squares, act_store, dve_norm, pe_turn = norm_blocks(
        nc, m, s, 0, x_all, x_all, h_t, m["B"][:, 0:D], [(s["x_loaded"], 48), (s["x_rest"], 16)])
    with nc.Block() as block:
        @block.sync
        def _(sp):
            x_rows = io["x"].rearrange("(b p) d -> p b d", p=P)
            sp.dma_start(x_all[:, 0:4, :], x_rows[:, 0:4, :]).then_inc(s["x_loaded"], 16)
            sp.dma_start(m["nrow"][:], io["norm_mix_row"]).then_inc(s["x_loaded"], 16)
            sp.dma_start(m["ident"][:], io["ident"]).then_inc(s["x_loaded"], 16)
            sp.dma_start(x_all[:, 4:8, :], x_rows[:, 4:8, :]).then_inc(s["x_rest"], 16)
            for c in range(2):
                sp.dma_start(w_v[c], io["w_v"][c]).then_inc(s[f"half_w{c}"], 16)
            sp.dma_start(m["col"][:, 0:TMP], io["cols"]).then_inc(s["consts"], 16)
            sp.dma_start(m["mask"][:], io["mask"]).then_inc(s["consts"], 16)
            sp.dma_start(m["keep"][:], io["keep"]).then_inc(s["consts"], 16)
            for i, name in enumerate("fgq"):
                sp.dma_start(seg(m["D"], 8192 + 1024 * i, 1024), io["w_hg"][0, :, 1024 * i:1024 * (i + 1)]
                             ).then_inc(s["w_" + name], 16)

        @block.tensor
        def _(pe):
            pe_turn(pe, 0)
            pe_turn(pe, 1)
            for n in range(2 * NB):
                c, b = n // NB, n % NB
                if b == 0:
                    pe.wait_ge(s[f"half_w{c}"], 16)
                if c == 0:
                    pe.wait_ge(s["stored"], b + 1)
                if n >= 4:
                    pe.wait_ge(s["v_stored"], n - 3)
                for k in range(KT):
                    last = nc.tensor.matmul(ps[:, 4 + n % 4, :], h_t[:, k, b * P:(b + 1) * P],
                                            w_v[c][:, k * 512:(k + 1) * 512], start=(k == 0), stop=(k == KT - 1))
                last.then_inc(s["half_psum"], 1)
                if c == 0 and b + 2 < NB:
                    pe_turn(pe, b + 2)

        @block.scalar
        def _(act):
            act_squares(act)
            act_store(act, 0)
            act_store(act, 1)
            for n in range(2 * NB):
                act.wait_ge(s["half_psum"], n + 1)
                nc.scalar.copy(v[:, n % NB, (n // NB) * 512:(n // NB + 1) * 512], ps[:, 4 + n % 4, :]
                               ).then_inc(s["v_stored"], 1)
                if n + 2 < NB:
                    act_store(act, n + 2)
            act.wait_ge(s["lb_max"], 2)
            nc.scalar.activation(col[:, TMP:TMP + 16], col[:, LBL:LBL + 16], ACT.Exp).then_inc(s["lb_exp"], 1)

        @block.vector
        def _(dve):
            dve_norm(dve)
            dve.wait_ge(s["consts"], 48)
            nc.vector.tensor_tensor(col[:, TMP:TMP + 8], col[:, LBL:LBL + 8], col[:, LBL + 8:LBL + 16],
                                    ALU.max).then_inc(s["lb_max0"], 1)
            dve.wait_ge(s["lb_max0"], 1)
            for r in range(2):
                nc.vector.tensor_tensor(col[:, LBL + 8 * r:LBL + 8 * r + 8], col[:, LBL + 8 * r:LBL + 8 * r + 8],
                                        col[:, TMP:TMP + 8], ALU.subtract).then_inc(s["lb_max"], 1)
            dve.wait_ge(s["lb_exp"], 1)
            nc.vector.tensor_tensor(col[:, LB:LB + 8], col[:, TMP:TMP + 8], col[:, TMP + 8:TMP + 16],
                                    ALU.add).then_inc(s["lb_step"], 1)
            dve.wait_ge(s["lb_step"], 1)
            nc.vector.reciprocal(col[:, OMLB:OMLB + 8], col[:, LB:LB + 8]).then_inc(s["lb_step"], 1)
            dve.wait_ge(s["lb_step"], 2)
            nc.vector.tensor_tensor(col[:, LB:LB + 8], col[:, TMP:TMP + 8], col[:, OMLB:OMLB + 8],
                                    ALU.mult).then_inc(s["lb_step"], 1)
            dve.wait_ge(s["lb_step"], 3)
            nc.vector.tensor_scalar(col[:, OMLB:OMLB + 8], col[:, LB:LB + 8], -1.0, 1.0, ALU.mult, ALU.add)


def hgrn(nc, m, s, io):
    h_t = seg(m["A"], 0, KT, T)
    v = seg(m["C"], 0, NB, HG_HEADS, P)
    mixed_t = seg(m["B"], 0, MT, T)
    w = seg(m["D"], 8192, 3, KT, P)
    f = seg(m["D"], 0, T)
    k = seg(m["D"], 1024, T)
    silu_g = seg(m["D"], 2048, T)
    G = seg(m["D"], 3072, T)
    eG = seg(m["D"], 4096, T)
    k_dec = seg(m["D"], 5120, T)
    k_end = seg(m["D"], 6144, T)
    q_dec = seg(m["D"], 7168, T)
    v_head = seg(m["D"], 11264, NB, P)
    o_normed = seg(m["D"], 12288, NB, P)
    k_nat = seg(m["D"], 13312, NB, P)
    scores = seg(m["D"], 14336, NB, P)
    state = seg(m["D"], 15360, NC, P)
    junk = seg(m["D"], 6144, NB, P)
    STEPS = NC - 1
    ps = m["ps"]
    col, ss = m["col"], m["ss"]
    fq_ps = ps[:, 0:2, :].rearrange("p a b -> p (a b)")
    g_ps = ps[:, 2:4, :].rearrange("p a b -> p (a b)")
    o_ps = ps[:, 4:6, :].rearrange("p u (b x) -> p (u b) x", b=4)
    oT_ps = ps[:, 4:6, :].rearrange("p a b -> p (a b)")

    def block_ps(bank, b):
        return ps[:, bank + b // 4, (b % 4) * P:(b % 4 + 1) * P]

    def sum_ps(j):
        return ps[:, 4 + j % 2 * 2 + j // 8, (j // 2 % 4) * P:(j // 2 % 4 + 1) * P]

    def bank_ps(bank):
        return ps[:, bank, :].rearrange("p (b x) -> p b x", b=4)

    def by_chunk(ap):
        return ap.rearrange("p (c t) -> p c t", t=C)

    with nc.Block() as block:
        @block.sync
        def _(sp):
            with sp.Fori(0, HG_HEADS - 1) as h:
                for i, name in enumerate("fgq"):
                    sp.wait_ge(s[name + "_psum"], h + 1)
                    sp.dma_start(seg(m["D"], 8192 + 1024 * i, 1024),
                                 io["w_hg"][bass.ds(h + 1, 1), :, 1024 * i:1024 * (i + 1)].rearrange("a p n -> p (a n)")
                                 ).then_inc(s["w_" + name], 16)

        @block.gpsimd
        def _(pool):
            def take_v(h):
                if not first(h):
                    pool.wait_ge(s["o_psum"], 2 * h)
                    pool.sem_inc(s["gate"], 1)
                nc.gpsimd.tensor_copy(v_head, v[:, :, bass.ds(h, 1), :].rearrange("p b a x -> p b (a x)")
                                      ).then_inc(s["v_head"], 1)
            take_v(0)
            with pool.Fori(1, HG_HEADS) as h:
                take_v(h)

        @block.tensor
        def _(pe):
            def product(dst, which):
                for u in range(2):
                    for kt in range(KT):
                        last = nc.tensor.matmul(dst[:, u * 512:(u + 1) * 512], w[:, which, kt, :],
                                                h_t[:, kt, u * 512:(u + 1) * 512], start=(kt == 0), stop=(kt == KT - 1))
                return last

            def project_f(h):
                pe.wait_ge(s["w_f"], 16 * (h + 1))
                if not first(h):
                    pe.wait_ge(s["q_copied"], h)
                product(fq_ps, 0).then_inc(s["f_psum"], 1)

            def project_g(h):
                pe.wait_ge(s["w_g"], 16 * (h + 1))
                if not first(h):
                    pe.wait_ge(s["silu_g"], h)
                product(g_ps, 1).then_inc(s["g_psum"], 1)

            def project_q(h):
                pe.wait_ge(s["w_q"], 16 * (h + 1))
                pe.wait_ge(s["f_sig"], h + 1)
                product(fq_ps, 2).then_inc(s["q_psum"], 1)

            def scores_and_keys(h):
                pe.wait_ge(s["q_dec"], h + 1)
                pe.wait_ge(s["k_dec"], h + 1)
                if not first(h):
                    pe.wait_ge(s["mixed"], h)
                for b in range(NB):
                    last = nc.tensor.matmul(block_ps(4, b), k_dec[:, b * P:(b + 1) * P],
                                            q_dec[:, b * P:(b + 1) * P], start=True, stop=True)
                last.then_inc(s["scores_psum"], 1)
                pe.wait_ge(s["k_end"], h + 1)
                for b in range(NB):
                    last = nc.tensor.transpose(block_ps(6, b), k_end[:, b * P:(b + 1) * P], m["ident"][:])
                last.then_inc(s["k_nat_psum"], 1)

            def sums(h):
                pe.wait_ge(s["v_head"], h + 1)
                pe.wait_ge(s["k_nat"], h + 1)
                pe.wait_ge(s["scores"], 2 * h + 2)
                for j in range(STEPS):
                    b, rows = j // 2, slice(j % 2 * C, (j % 2 + 1) * C)
                    last = nc.tensor.matmul(sum_ps(j), k_nat[rows, b, :], v_head[rows, b, :], start=True, stop=True)
                    if j == 7 or j == STEPS - 1:
                        last.then_inc(s["sums_psum"], 1)

            def outputs(h):
                pe.wait_ge(s["state_zero"], 1)
                for b in range(NB):
                    if b % 4 == 0:
                        pe.wait_ge(s["state"], STEPS * h + (8 if b == 0 else STEPS))
                    nc.tensor.matmul(o_ps[:, b, :], scores[:, b, :], v_head[:, b, :], start=True, stop=False,
                                     skip_group_check=True)
                    for c in range(2):
                        j = 2 * b + c
                        last = nc.tensor.matmul(o_ps[c * C:(c + 1) * C, b, :], q_dec[:, j * C:(j + 1) * C],
                                                state[:, j, :], start=False, stop=True, skip_group_check=True)
                    if b % 4 == 3:
                        last.then_inc(s["o_psum"], 1)

            def turn(h):
                pe.wait_ge(s["o_normed"], h + 1)
                for b in range(NB):
                    last = nc.tensor.transpose(oT_ps[:, b * P:(b + 1) * P], o_normed[:, b, :], m["ident"][:])
                last.then_inc(s["oT_psum"], 1)

            project_f(0)
            project_g(0)
            project_q(0)
            project_f(1)
            with pe.Fori(0, HG_HEADS - 2) as h:
                scores_and_keys(h)
                project_g(h + 1)
                sums(h)
                project_q(h + 1)
                outputs(h)
                project_f(h + 2)
                turn(h)
            scores_and_keys(HG_HEADS - 2)
            project_g(HG_HEADS - 1)
            sums(HG_HEADS - 2)
            project_q(HG_HEADS - 1)
            outputs(HG_HEADS - 2)
            turn(HG_HEADS - 2)
            scores_and_keys(HG_HEADS - 1)
            sums(HG_HEADS - 1)
            outputs(HG_HEADS - 1)
            turn(HG_HEADS - 1)

        @block.scalar
        def _(act):
            def forget_gate(h):
                act.wait_ge(s["f_psum"], h + 1)
                if not first(h):
                    act.wait_ge(s["G"], h)
                nc.scalar.activation(f, fq_ps, ACT.Sigmoid).then_inc(s["f_sig"], 1)

            def queries_and_log(h):
                act.wait_ge(s["q_psum"], h + 1)
                if not first(h):
                    act.wait_ge(s["o_psum"], 2 * h)
                nc.scalar.copy(q_dec, fq_ps).then_inc(s["q_copied"], 1)
                act.wait_ge(s["f"], h + 1)
                act.wait_ge(s["k"], h + 1)
                nc.scalar.activation(f, f, ACT.Ln).then_inc(s["log_f"], 1)

            def head(h, more=True):
                act.wait_ge(s["G"], h + 1)
                if not first(h):
                    act.wait_ge(s["state"], STEPS * h)
                nc.scalar.activation(eG, G, ACT.Exp).then_inc(s["eG"], 1)
                if not first(h):
                    act.wait_ge(s["scores_psum"], h)
                nc.scalar.activation(k_dec, G, ACT.Exp, scale=-1.0).then_inc(s["emG"], 1)
                act.wait_ge(s["to_end"], h + 1)
                nc.scalar.activation(k_end, k_end, ACT.Exp).then_inc(s["e_end"], 1)
                act.wait_ge(s["g_psum"], h + 1)
                if not first(h):
                    act.wait_ge(s["mixed"], h)
                nc.scalar.activation(silu_g, g_ps, ACT.Sigmoid).then_inc(s["g_sig"], 1)
                act.wait_ge(s["k_nat_psum"], h + 1)
                if not first(h):
                    act.wait_ge(s["sums_psum"], 2 * h)
                nc.scalar.copy(k_nat, ps[:, 6:8, :].rearrange("p u (b x) -> p (u b) x", b=4)).then_inc(s["k_nat"], 1)
                if more:
                    forget_gate(h + 1)
                    queries_and_log(h + 1)
                for b in range(NB):
                    if b % 4 == 0:
                        act.wait_ge(s["o_psum"], 2 * h + b // 4 + 1)
                    nc.scalar.activation(junk[:, b, :], o_ps[:, b, :], ACT.Square, accum_out=ss[:, b:b + 1]
                                         ).then_inc(s["o_squared"], 1)
                act.wait_ge(s["o_mean"], h + 1)
                nc.scalar.activation(ss[:, 8:16], ss[:, 8:16], ACT.Sqrt).then_inc(s["o_root"], 1)

            forget_gate(0)
            queries_and_log(0)
            head(0)
            with act.Fori(1, HG_HEADS - 1) as h:
                head(h)
            head(HG_HEADS - 1, more=False)

        @block.vector
        def _(dve):
            nc.vector.memset(scores, 0.0).then_inc(s["scores_zero"], 1)
            nc.vector.memset(state[:, 0, :], 0.0).then_inc(s["state_zero"], 1)
            dve.wait_ge(s["scores_zero"], 1)

            def forget_gate(h):
                dve.wait_ge(s["f_sig"], h + 1)
                nc.vector.tensor_scalar(f, f, col[:, bass.ds(h + OMLB, 1)], col[:, bass.ds(h + LB, 1)],
                                        ALU.mult, ALU.add).then_inc(s["f"], 1)
                dve.wait_ge(s["f"], h + 1)
                nc.vector.tensor_scalar(k, f, -1.0, 1.0, ALU.mult, ALU.add).then_inc(s["k"], 1)

            def sum_log(h):
                dve.wait_ge(s["log_f"], h + 1)
                nc.vector.tensor_tensor_scan(G, m["keep"][:], f, 0.0, ALU.mult, ALU.add).then_inc(s["G"], 1)

            def to_end(h):
                dve.wait_ge(s["G"], h + 1)
                if not first(h):
                    dve.wait_ge(s["o_squared"], NB * h)
                nc.vector.tensor_tensor(by_chunk(k_end), by_chunk(G)[:, :, C - 1:C].to_broadcast([P, NC, C]),
                                        by_chunk(G), ALU.subtract).then_inc(s["to_end"], 1)

            def head(h, more=True):
                dve.wait_ge(s["eG"], h + 1)
                dve.wait_ge(s["q_copied"], h + 1)
                nc.vector.tensor_tensor(q_dec, q_dec, eG, ALU.mult).then_inc(s["q_dec"], 1)
                dve.wait_ge(s["emG"], h + 1)
                nc.vector.tensor_tensor(k_dec, k_dec, k, ALU.mult).then_inc(s["k_dec"], 1)
                dve.wait_ge(s["e_end"], h + 1)
                nc.vector.tensor_tensor(k_end, k_end, k, ALU.mult).then_inc(s["k_end"], 1)
                dve.wait_ge(s["g_sig"], h + 1)
                nc.vector.tensor_tensor(silu_g, silu_g, g_ps, ALU.mult).then_inc(s["silu_g"], 1)
                dve.wait_ge(s["scores_psum"], h + 1)
                dve.sem_inc(s["gate"], 1)
                for u in range(2):
                    nc.vector.copy_predicated(scores[:, 4 * u:4 * u + 4, :],
                                              m["mask"][:].unsqueeze(1).to_broadcast([P, 4, P]), bank_ps(4 + u)
                                              ).then_inc(s["scores"], 1)
                for j in range(STEPS):
                    if j % 8 == 0:
                        dve.wait_ge(s["sums_psum"], 2 * h + j // 8 + 1)
                    if j > 0:
                        dve.wait_ge(s["state"], STEPS * h + j)
                    nc.vector.scalar_tensor_tensor(
                        out=state[:, j + 1, :], in0=state[:, j, :], scalar=eG[:, j * C + C - 1:j * C + C],
                        in1=sum_ps(j), op0=ALU.mult, op1=ALU.add
                        ).then_inc(s["state"], 1)
                if more:
                    forget_gate(h + 1)
                    sum_log(h + 1)
                dve.wait_ge(s["o_squared"], NB * (h + 1))
                nc.vector.tensor_scalar(ss[:, 8:16], ss[:, 0:8], 1.0 / P, EPS, ALU.mult, ALU.add).then_inc(s["o_mean"], 1)
                dve.wait_ge(s["o_root"], h + 1)
                nc.vector.reciprocal(ss[:, 16:24], ss[:, 8:16]).then_inc(s["o_rstd"], 1)
                dve.wait_ge(s["o_rstd"], h + 1)
                nc.vector.tensor_tensor(o_normed, o_ps, ss[:, 16:24].unsqueeze(2).to_broadcast([P, NB, P]),
                                        ALU.mult).then_inc(s["o_normed"], 1)
                if more:
                    to_end(h + 1)
                dve.wait_ge(s["oT_psum"], h + 1)
                nc.vector.scalar_tensor_tensor(
                    out=mixed_t[:, bass.ds(h, 1), :].rearrange("p a t -> p (a t)"), in0=oT_ps,
                    scalar=col[:, HGW:HGW + 1], in1=silu_g, op0=ALU.mult, op1=ALU.mult).then_inc(s["mixed"], 1)

            forget_gate(0)
            sum_log(0)
            to_end(0)
            head(0)
            with dve.Fori(1, HG_HEADS - 1) as h:
                head(h)
            head(HG_HEADS - 1, more=False)


def project_z(nc, m, s, io):
    h_t = seg(m["A"], 0, KT, T)
    z = seg(m["C"], 0, NB, D)
    with nc.Block() as block:
        @block.sync
        def _(sp):
            for c in range(2):
                sp.dma_start(seg(m["B"], 8192 + 4096 * c, 4096), io["w_z"][c]).then_inc(s[f"half_w{c}"], 16)
            for u in range(2):
                sp.dma_start(seg(m["D"], 12288 + 1024 * u, 1024), io["w_xbc"][u]).then_inc(s[f"w_xbc{u}"], 16)

        @block.tensor
        def _(pe):
            for n in range(2 * NB):
                c, b = n // NB, n % NB
                if b == 0:
                    pe.wait_ge(s[f"half_w{c}"], 32)
                if n >= 4:
                    pe.wait_ge(s["z_stored"], n - 3)
                for k in range(KT):
                    last = nc.tensor.matmul(m["ps"][:, n % 4, :], h_t[:, k, b * P:(b + 1) * P],
                                            m["B"][:, 8192 + 4096 * c + 512 * k:8192 + 4096 * c + 512 * (k + 1)],
                                            start=(k == 0), stop=(k == KT - 1))
                last.then_inc(s["half_psum"], 1)

        @block.scalar
        def _(act):
            for n in range(16):
                act.wait_ge(s["half_psum"], 16 + n + 1)
                nc.scalar.activation(z[:, n % NB, (n // NB) * 512:(n // NB + 1) * 512], m["ps"][:, n % 4, :],
                                     ACT.Sigmoid).then_inc(s["z_sig"], 1)

        @block.vector
        def _(dve):
            for n in range(16):
                part = z[:, n % NB, (n // NB) * 512:(n // NB + 1) * 512]
                dve.wait_ge(s["z_sig"], n + 1)
                nc.vector.tensor_tensor(part, part, m["ps"][:, n % 4, :], ALU.mult).then_inc(s["z_stored"], 1)


XBC = 0
SEL = 12288
SSN = 14336
DECAY = 14848
CUM = 15104


def project_xbc(nc, m, s, io):
    h_t = seg(m["A"], 0, KT, T)
    xbc = seg(m["D"], XBC, CT, T)
    w = [seg(m["D"], SEL + 1024 * u, KT, P) for u in range(2)]
    raw = [seg(m["B"], 8192 + 1027 * u, TAPS - 1 + T) for u in range(2)]
    sig = seg(m["B"], 10246, T)
    w_dt = seg(m["B"], 11270, KT, SSD_HEADS)
    H = SSD_HEADS
    dt, t1, eC = (m["B"][0:H, 11398 + 1024 * u:12422 + 1024 * u] for u in range(3))
    diag = m["B"][0:H, 14470:14726].rearrange("p (c h) -> p c h", h=H)
    ones = m["B"][0:H, 14726:14854]
    cum = m["D"][0:H, CUM:CUM + T]
    col, ps, keep = m["col"], m["ps"], m["keep"]
    dt_ps = ps[0:H, 4:6, :].rearrange("p a b -> p (a b)")

    def by_chunk(ap):
        return ap.rearrange("p (c t) -> p c t", t=C)

    with nc.Block() as block:
        @block.sync
        def _(sp):
            sp.dma_start(seg(m["B"], 11270, KT * H), io["w_dt"]).then_inc(s["w_dt"], 16)
            with sp.Fori(0, CT // 2 - 1) as i:
                for u in range(2):
                    sp.wait_ge(s["xbc_psum"], 2 * i + u + 1)
                    sp.dma_start(seg(m["D"], SEL + 1024 * u, 1024), io["w_xbc"][bass.ds(2 * i + u + 2, 1)].rearrange(
                        "a p n -> p (a n)")).then_inc(s[f"w_xbc{u}"], 16)

        @block.tensor
        def _(pe):
            pe.wait_ge(s["w_dt"], 16)
            for u in range(2):
                for kt in range(KT):
                    last = nc.tensor.matmul(dt_ps[:, u * 512:(u + 1) * 512], w_dt[:, kt, :],
                                            h_t[:, kt, u * 512:(u + 1) * 512], start=(kt == 0), stop=(kt == KT - 1))
            last.then_inc(s["dt_psum"], 1)

            def tile(i, u):
                n = 2 * i + u
                pe.wait_ge(s[f"w_xbc{u}"], 16 * (i + 1))
                if not first(i):
                    pe.wait_ge(s["raw"], n - 1)
                for t in range(2):
                    for kt in range(KT):
                        last = nc.tensor.matmul(ps[:, 2 * u + t, :], w[u][:, kt, :], h_t[:, kt, t * 512:(t + 1) * 512],
                                                start=(kt == 0), stop=(kt == KT - 1))
                last.then_inc(s["xbc_psum"], 1)

            tile(0, 0)
            tile(0, 1)
            for q, (rows, ready, count) in enumerate(((dt, "dt", 1), (cum, "cum", 1), (eC, "eC", 1), (t1, "dt_end", 1))):
                pe.wait_ge(s[ready], count)
                for b in range(NB):
                    last = nc.tensor.transpose(ps[:, 6, (4 * b + q) * H:(4 * b + q + 1) * H],
                                               rows[:, b * P:(b + 1) * P], m["ident"][0:H, 0:H])
            last.then_inc(s["nat_psum"], 1)
            pe.wait_ge(s["diag"], 1)
            pe.wait_ge(s["ones"], 1)
            nc.tensor.matmul(ps[:, 7, 0:NC * H], ones, m["B"][0:H, 14470:14726], start=True, stop=True
                             ).then_inc(s["decay_psum"], 1)
            with pe.Fori(1, CT // 2) as i:
                tile(i, 0)
                tile(i, 1)

        @block.scalar
        def _(act):
            act.wait_ge(s["dt_abs"], 1)
            nc.scalar.activation(t1, t1, ACT.Exp, scale=-1.0).then_inc(s["dt_exp"], 1)
            act.wait_ge(s["dt_exp"], 1)
            nc.scalar.activation(t1, t1, ACT.Ln, bias=1.0).then_inc(s["dt_log"], 1)
            nc.scalar.activation(col[0:H, SSDH + 2:SSDH + 3], col[0:H, SSDH + 1:SSDH + 2], ACT.Exp).then_inc(s["A_exp"], 1)
            act.wait_ge(s["cum"], 1)
            nc.scalar.activation(eC, cum, ACT.Exp).then_inc(s["eC"], 1)
            act.wait_ge(s["c_end"], 1)
            nc.scalar.activation(t1, t1, ACT.Exp).then_inc(s["e_c_end"], 1)
            act.wait_ge(s["nat_psum"], 1)
            nc.scalar.copy(seg(m["D"], SSN, 512), ps[:, 6, :])
            act.wait_ge(s["decay_psum"], 1)
            nc.scalar.copy(seg(m["D"], DECAY, 256), ps[:, 7, 0:256])

            def tile(i, u):
                n = 2 * i + u
                act.wait_ge(s["xbc_psum"], n + 1)
                if not first(i):
                    act.wait_ge(s["conv"], TAPS * (n - 1))
                nc.scalar.copy(raw[u][:, TAPS - 1:], ps[:, 2 * u:2 * u + 2, :].rearrange("p a b -> p (a b)")
                               ).then_inc(s["raw"], 1)
                act.wait_ge(s["conv"], TAPS * (n + 1))
                if not (first(i) and u == 0):
                    act.wait_ge(s["xbc"], n)
                nc.scalar.activation(sig, xbc[:, bass.ds(n, 1), :].rearrange("p a t -> p (a t)"), ACT.Sigmoid
                                     ).then_inc(s["xbc_sig"], 1)
            tile(0, 0)
            tile(0, 1)
            with act.Fori(1, CT // 2) as i:
                tile(i, 0)
                tile(i, 1)

        @block.vector
        def _(dve):
            for u in range(2):
                nc.vector.memset(raw[u][:, 0:TAPS - 1], 0.0).then_inc(s["raw_zero"], 1)
            nc.vector.memset(ones, 1.0).then_inc(s["ones"], 1)
            dve.wait_ge(s["dt_psum"], 1)
            nc.vector.tensor_scalar(dt, dt_ps, col[0:H, SSDH:SSDH + 1], None, ALU.add).then_inc(s["dt_raw"], 1)
            dve.wait_ge(s["dt_raw"], 1)
            nc.vector.scalar_tensor_tensor(out=t1, in0=dt, scalar=-1.0, in1=dt, op0=ALU.mult, op1=ALU.max).then_inc(s["dt_abs"], 1)
            dve.wait_ge(s["dt_log"], 1)
            nc.vector.scalar_tensor_tensor(out=dt, in0=dt, scalar=0.0, in1=t1, op0=ALU.max, op1=ALU.add
                                           ).then_inc(s["dt"], 1)
            dve.wait_ge(s["dt"], 1)
            dve.wait_ge(s["A_exp"], 1)
            nc.vector.tensor_scalar(t1, dt, col[0:H, SSDH + 2:SSDH + 3], -1.0, ALU.mult, ALU.mult).then_inc(s["dA"], 1)
            dve.wait_ge(s["dA"], 1)
            nc.vector.tensor_tensor_scan(cum, keep[0:H, :], t1, 0.0, ALU.mult, ALU.add).then_inc(s["cum"], 1)
            dve.wait_ge(s["cum"], 1)
            nc.vector.tensor_tensor(by_chunk(t1), by_chunk(cum)[:, :, C - 1:C].to_broadcast([H, NC, C]), by_chunk(cum),
                                    ALU.subtract).then_inc(s["c_end"], 1)
            dve.wait_ge(s["e_c_end"], 1)
            nc.vector.tensor_tensor(t1, t1, dt, ALU.mult).then_inc(s["dt_end"], 1)
            dve.wait_ge(s["eC"], 1)
            nc.vector.tensor_tensor(diag, by_chunk(eC)[:, :, C - 1:C].to_broadcast([H, NC, H]),
                                    m["ident"][0:H, 0:H].unsqueeze(1).to_broadcast([H, NC, H]),
                                    ALU.mult).then_inc(s["diag"], 1)
            dve.wait_ge(s["raw_zero"], 2)

            def tile(i, u):
                n = 2 * i + u
                out = xbc[:, bass.ds(n, 1), :].rearrange("p a t -> p (a t)")
                dve.wait_ge(s["raw"], n + 1)
                nc.vector.tensor_scalar(out, raw[u][:, 0:T], col[:, bass.ds(CONVW + n * TAPS, 1)],
                                        col[:, bass.ds(CONVB + n, 1)], ALU.mult, ALU.add).then_inc(s["conv"], 1)
                for j in range(1, TAPS):
                    dve.wait_ge(s["conv"], TAPS * n + j)
                    nc.vector.scalar_tensor_tensor(out=out, in0=raw[u][:, j:j + T],
                                                   scalar=col[:, bass.ds(CONVW + n * TAPS + j, 1)], in1=out,
                                                   op0=ALU.mult, op1=ALU.add).then_inc(s["conv"], 1)
                dve.wait_ge(s["xbc_sig"], n + 1)
                nc.vector.tensor_tensor(out, out, sig, ALU.mult).then_inc(s["xbc"], 1)
            tile(0, 0)
            tile(0, 1)
            with dve.Fori(1, CT // 2) as i:
                tile(i, 0)
                tile(i, 1)


def ssd(nc, m, s, io):
    H, SP = SSD_HEADS, SSD_P
    xbc = seg(m["D"], XBC, CT, T)
    sel = m["D"][0:H, SEL:SEL + H * P].rearrange("p (h x) -> p h x", h=H)
    ssn = seg(m["D"], SSN, 4 * NB, H)
    decay = seg(m["D"], DECAY, NC, H)
    cum = m["D"][0:H, CUM:CUM + T]
    z = seg(m["C"], 0, NB, D)
    mixed_t = seg(m["B"], 0, MT, T)
    xb = seg(m["A"], 0, CT, P)
    xs = seg(m["A"], 1536, H, SP)
    xdt = seg(m["A"], 2560, H, SP)
    xend = seg(m["A"], 3584, H, SP)
    L = seg(m["A"], 4608, H, P)
    b_nat = seg(m["A"], 6656, 2, P)
    cb = seg(m["A"], 6912, 2, P)
    state = seg(m["A"], 7168, H, SP)
    y = seg(m["D"], 16128, H, SP)
    y_flat = seg(m["D"], 16128, D)
    SUM_BANK = (7, 0)
    col, ps, ss = m["col"], m["ps"], m["ss"]

    def heads(lo):
        return ps[:, lo:lo + 2, :].rearrange("p u (h x) -> p (u h) x", x=SP)

    def of_block(b, q):
        return ssn[:, bass.ds(4 * b + q, 1), :].rearrange("p a h -> p (a h)")

    with nc.Block() as block:
        @block.sync
        def _(sp):
            sp.dma_start(m["D"][0:H, SEL:SEL + H * P], io["sel"]).then_inc(s["sel"], 16)

        @block.gpsimd
        def _(pool):
            def take(b):
                if not first(b):
                    pool.wait_ge(s["yoff_psum"], 2 * b)
                    pool.sem_inc(s["gate"], 1)
                nc.gpsimd.tensor_copy(xb, xbc[:, :, bass.ds(b * P, P)]).then_inc(s["xb"], 1)

            def scale_x(b):
                pool.wait_ge(s["xs"], b + 1)
                pool.sem_inc(s["gate"], 1)
                if not first(b):
                    pool.wait_ge(s["sum_psum"], 4 * b)
                    pool.sem_inc(s["gate"], 1)
                nc.gpsimd.tensor_tensor(xend, xs, of_block(b, 3).unsqueeze(2).to_broadcast([P, H, SP]), ALU.mult
                                        ).then_inc(s["xend"], 1)
                pool.wait_ge(s["xend"], b + 1)
                pool.sem_inc(s["gate"], 1)
                pool.wait_ge(s["xdt"], b + 1)
                pool.sem_inc(s["gate"], 1)
                nc.gpsimd.tensor_tensor(xs, xs, col[:, DROW:DROW + H].unsqueeze(2).to_broadcast([P, H, SP]), ALU.mult
                                        ).then_inc(s["x_skip"], 1)
            take(0)
            scale_x(0)
            with pool.Fori(1, NB) as b:
                take(b)
                scale_x(b)

        @block.tensor
        def _(pe):
            pe.wait_ge(s["sel"], 16)

            def prepare(b):
                pe.wait_ge(s["xb"], b + 1)
                if not first(b):
                    pe.wait_ge(s["ssd_state"], 4 * b + 1)
                for c in range(8):
                    last = nc.tensor.transpose(ps[:, c // 4, (c % 4) * P:(c % 4 + 1) * P], xb[:, c, :], m["ident"][:])
                last.then_inc(s["xs_psum"], 1)
                if not first(b):
                    pe.wait_ge(s["cb"], 2 * b)
                for g in range(2):
                    nc.tensor.transpose(ps[:, 2, g * P:(g + 1) * P], xb[:, 8 + g, :], m["ident"][:])
                for g in range(2):
                    last = nc.tensor.matmul(ps[:, 2, (2 + g) * P:(3 + g) * P], xb[:, 8 + g, :], xb[:, 10 + g, :],
                                            start=True, stop=True)
                last.then_inc(s["b_psum"], 1)
                for g in range(2):
                    if g == 1:
                        pe.wait_ge(s["diff"], 3 * b + 1)
                    elif not first(b):
                        pe.wait_ge(s["y_off"], b)
                    if g == 1 or not first(b):
                        pe.sem_inc(s["gate"], 1)
                    for i in range(8):
                        last = nc.tensor.matmul(ps[:, 3 + i // 4, (i % 4) * P:(i % 4 + 1) * P], sel[:, 8 * g + i, :],
                                                cum[:, bass.ds(b * P, P)], start=True, stop=True)
                    last.then_inc(s["row_psum"], 1)

            def combine(b):
                pe.wait_ge(s["diff"], 3 * b + 2)
                for c in range(2):
                    pe.wait_ge(s["ssd_state"], 4 * b + 2 * c + 1)
                    for g in range(2):
                        last = nc.tensor.matmul(ps[c * C:(c + 1) * C, 3 + g, :], xb[:, 10 + g, c * C:(c + 1) * C],
                                                state[:, g * 8:(g + 1) * 8, :], start=True, stop=True)
                    last.then_inc(s["yoff_psum"], 1)
                    if c == 0:
                        pe.wait_ge(s["b_nat"], b + 1)
                        pe.wait_ge(s["xend"], b + 1)
                    for g in range(2):
                        nc.tensor.matmul(ps[:, SUM_BANK[g], :], b_nat[c * C:(c + 1) * C, g, :],
                                         xend[c * C:(c + 1) * C, g * 8:(g + 1) * 8, :], start=True, stop=True
                                         ).then_inc(s["sum_psum"], 1)
                pe.wait_ge(s["weights"], b + 1)
                pe.wait_ge(s["xdt"], b + 1)
                if not first(b):
                    pe.wait_ge(s["y_mixed"], b)
                for h in range(H):
                    last = nc.tensor.matmul(ps[:, 5 + h // 8, (h % 8) * SP:(h % 8 + 1) * SP], L[:, h, :], xdt[:, h, :],
                                            start=True, stop=True)
                last.then_inc(s["ydiag_psum"], 1)

            def turn(b):
                pe.wait_ge(s["y_normed"], 2 * b + 2)
                for c in range(8):
                    last = nc.tensor.transpose(ps[:, 5 + c // 4, (c % 4) * P:(c % 4 + 1) * P],
                                               y_flat[:, c * P:(c + 1) * P], m["ident"][:])
                last.then_inc(s["yT_psum"], 1)

            def blk(b):
                combine(b)
                prepare(b + 1)
                turn(b)
            prepare(0)
            blk(0)
            with pe.Fori(1, NB - 1) as b:
                blk(b)
            combine(NB - 1)
            turn(NB - 1)

        @block.scalar
        def _(act):
            def take(b):
                act.wait_ge(s["xs_psum"], b + 1)
                if not first(b):
                    act.wait_ge(s["y_skip"], b)
                nc.scalar.copy(xs, heads(0)).then_inc(s["xs"], 1)
                act.wait_ge(s["b_psum"], b + 1)
                if not first(b):
                    act.wait_ge(s["sum_psum"], 4 * b)
                nc.scalar.copy(b_nat, ps[:, 2, 0:2 * P].rearrange("p (g x) -> p g x", g=2)).then_inc(s["b_nat"], 1)

            def decays(b):
                act.wait_ge(s["diff"], 3 * b + 3)
                nc.scalar.activation(L, L, ACT.Exp).then_inc(s["L"], 1)

            def blk(b, more=True):
                act.wait_ge(s["y_gated"], b + 1)
                for g in range(2):
                    part = slice(g * 512, (g + 1) * 512)
                    nc.scalar.activation(m["nrow"][:, part], y_flat[:, part], ACT.Square,
                                         accum_out=ss[:, g:g + 1]).then_inc(s["y_squared"], 1)
                if more:
                    take(b + 1)
                act.wait_ge(s["y_mean"], b + 1)
                nc.scalar.activation(ss[:, 2:4], ss[:, 2:4], ACT.Sqrt).then_inc(s["y_root"], 1)
                act.wait_ge(s["y_rstd"], b + 1)
                for g in range(2):
                    part = y_flat[:, g * 512:(g + 1) * 512]
                    nc.scalar.activation(part, part, ACT.Copy, scale=ss[:, 4 + g:5 + g]).then_inc(s["y_normed"], 1)
                if more:
                    decays(b + 1)
            take(0)
            decays(0)
            blk(0)
            with act.Fori(1, NB - 1) as b:
                blk(b)
            blk(NB - 1, more=False)

        @block.vector
        def _(dve):
            nc.vector.memset(cb, 0.0).then_inc(s["cb_zero"], 1)
            nc.vector.memset(state, 0.0).then_inc(s["ssd_state"], 1)
            dve.wait_ge(s["cb_zero"], 1)

            def over_channels(b, q):
                return of_block(b, q).unsqueeze(2).to_broadcast([P, H, SP])

            def differences(b):
                if not first(b):
                    dve.wait_ge(s["ydiag_psum"], b)
                for g in range(2):
                    dve.wait_ge(s["row_psum"], 2 * b + g + 1)
                    nc.vector.tensor_tensor(L[:, g * 8:(g + 1) * 8, :],
                                            ps[:, 3:5, :].rearrange("p u (h x) -> p (u h) x", x=P),
                                            of_block(b, 1)[:, g * 8:(g + 1) * 8].unsqueeze(2).to_broadcast([P, 8, P]),
                                            ALU.subtract).then_inc(s["diff"], 1)

            def inputs(b):
                dve.wait_ge(s["diff"], 3 * b + 2)
                nc.vector.tensor_scalar(L, L, 0.0, None, ALU.min).then_inc(s["diff"], 1)
                dve.wait_ge(s["xs"], b + 1)
                nc.vector.tensor_tensor(xdt, xs, over_channels(b, 0), ALU.mult).then_inc(s["xdt"], 1)
                dve.wait_ge(s["b_psum"], b + 1)
                dve.wait_ge(s["b_nat"], b + 1)
                if not first(b):
                    dve.wait_ge(s["weights"], b)
                dve.sem_inc(s["gate"], 1)
                for g in range(2):
                    nc.vector.copy_predicated(cb[:, g, :], m["mask"][:], ps[:, 2, (2 + g) * P:(3 + g) * P]
                                              ).then_inc(s["cb"], 1)

            def update_state(b, c):
                dve.wait_ge(s["yoff_psum"], 2 * b + c + 1)
                for g in range(2):
                    part = state[:, g * 8:(g + 1) * 8, :]
                    dve.wait_ge(s["ssd_state"], 4 * b + 2 * c + 1)
                    nc.vector.tensor_tensor(part, part, decay[:, bass.ds(2 * b + c, 1), g * 8:(g + 1) * 8].rearrange(
                        "p a h -> p (a h)").unsqueeze(2).to_broadcast([P, 8, SP]), ALU.mult).then_inc(s["decayed"], 1)
                for g in range(2):
                    part = state[:, g * 8:(g + 1) * 8, :]
                    dve.wait_ge(s["decayed"], 4 * b + 2 * c + g + 1)
                    dve.wait_ge(s["sum_psum"], 4 * b + 2 * c + g + 1)
                    nc.vector.tensor_tensor(part, part, ps[:, SUM_BANK[g], :].rearrange("p (h x) -> p h x", x=SP),
                                            ALU.add).then_inc(s["ssd_state"], 1)

            def outputs(b):
                dve.wait_ge(s["L"], b + 1)
                dve.wait_ge(s["cb"], 2 * b + 2)
                for g in range(2):
                    part = L[:, g * 8:(g + 1) * 8, :]
                    last = nc.vector.tensor_tensor(part, part, cb[:, g:g + 1, :].to_broadcast([P, 8, P]), ALU.mult)
                last.then_inc(s["weights"], 1)
                update_state(b, 0)
                dve.wait_ge(s["yoff_psum"], 2 * b + 2)
                if not first(b):
                    dve.wait_ge(s["yT_psum"], b)
                nc.vector.tensor_tensor(y, heads(3), over_channels(b, 2), ALU.mult).then_inc(s["y_off"], 1)
                update_state(b, 1)
                dve.wait_ge(s["y_off"], b + 1)
                dve.wait_ge(s["ydiag_psum"], b + 1)
                nc.vector.tensor_tensor(y, y, heads(5), ALU.add).then_inc(s["y_sum"], 1)
                dve.wait_ge(s["y_sum"], b + 1)
                dve.wait_ge(s["x_skip"], b + 1)
                nc.vector.tensor_tensor(y, y, xs, ALU.add).then_inc(s["y_skip"], 1)
                dve.wait_ge(s["y_skip"], b + 1)
                nc.vector.tensor_tensor(y_flat, y_flat, z[:, bass.ds(b, 1), :].rearrange("p a d -> p (a d)"),
                                        ALU.mult).then_inc(s["y_gated"], 1)

            def mean(b):
                dve.wait_ge(s["y_squared"], 2 * b + 2)
                nc.vector.tensor_scalar(ss[:, 2:4], ss[:, 0:2], 1.0 / 512, EPS, ALU.mult, ALU.add).then_inc(s["y_mean"], 1)

            def store(b):
                dve.wait_ge(s["y_root"], b + 1)
                nc.vector.reciprocal(ss[:, 4:6], ss[:, 2:4]).then_inc(s["y_rstd"], 1)
                dve.wait_ge(s["yT_psum"], b + 1)
                nc.vector.tensor_tensor(mixed_t[:, 8:16, bass.ds(b * P, P)],
                                        ps[:, 5:7, :].rearrange("p u (c t) -> p (u c) t", c=4),
                                        col[:, SSDW:SSDW + 8].unsqueeze(2).to_broadcast([P, 8, P]),
                                        ALU.mult).then_inc(s["y_mixed"], 1)

            def blk(b):
                outputs(b)
                differences(b + 1)
                mean(b)
                inputs(b + 1)
                store(b)
            differences(0)
            inputs(0)
            blk(0)
            with dve.Fori(1, NB - 1) as b:
                blk(b)
            outputs(NB - 1)
            mean(NB - 1)
            store(NB - 1)


WQ, QT, KEYS = 8192, 10240, 12288
SC, CAND, ONEHOT = 12544, 13056, 13312
TOPV, TOPF, BESTV, GATE = 13824, 13856, 13888, 14016
ACTV, IDS, DIAG = 14144, 14208, 14336


def project_out(nc, m, s, io):
    mixed_t = seg(m["B"], 0, MT, T)
    h2_t = seg(m["B"], 0, KT, T)
    x2 = seg(m["A"], 0, NB, D)
    h2 = seg(m["C"], 0, NB, D)
    w = [seg(m["D"], 8192 * c, MT, 512) for c in range(2)]
    junk = m["keep"][:]
    ps, ss = m["ps"], m["ss"]
    order = [(0, 0), (1, 0), (0, 1), (1, 1)] + [(b, c) for b in range(2, NB) for c in range(2)]
    PARTS = 4
    with nc.Block() as block:
        @block.sync
        def _(sp):
            for i in range(PARTS):
                sp.dma_start(seg(m["D"], 2048 * i, 2048), io["w_out"][0, :, 2048 * i:2048 * (i + 1)]
                             ).then_inc(s[f"w_out{i}"], 16)
            sp.dma_start(seg(m["D"], 8192, 8192), io["w_out"][1]).then_inc(s["half_w1"], 16)
            sp.dma_start(x2, io["x"].rearrange("(b p) d -> p b d", p=P)).then_inc(s["x_again"], 16)
            sp.dma_start(m["nrow"][:], io["norm_ffn_row"]).then_inc(s["ffn_row"], 16)

        @block.tensor
        def _(pe):
            def turn(b):
                pe.wait_ge(s["normed"], NB + b + 1)
                if b >= 2:
                    pe.wait_ge(s["stored"], NB + b - 1)
                for k in range(KT):
                    last = nc.tensor.transpose(ps[:, 4 + 2 * (b % 2) + k // 4, (k % 4) * P:(k % 4 + 1) * P],
                                               h2[:, b, k * P:(k + 1) * P], m["ident"][:])
                last.then_inc(s["turned"], 1)

            for n, (b, c) in enumerate(order):
                if n == 2:
                    pe.wait_ge(s["half_w1"], 48)
                if n >= 4:
                    pe.wait_ge(s["x2"], n - 3)
                for k in range(MT):
                    if n == 0 and k % (MT // PARTS) == 0:
                        pe.wait_ge(s[f"w_out{k // (MT // PARTS)}"], 16)
                    last = nc.tensor.matmul(ps[:, n % 4, :], mixed_t[:, k, b * P:(b + 1) * P], w[c][:, k, :],
                                            start=(k == 0), stop=(k == MT - 1))
                last.then_inc(s["half_psum"], 1)
                if n % 2 == 1 and n >= 5:
                    turn(b - 2)
            turn(NB - 2)
            turn(NB - 1)

        @block.scalar
        def _(act):
            def store(b):
                act.wait_ge(s["turned"], NB + b + 1)
                nc.scalar.copy(h2_t[:, :, b * P:(b + 1) * P],
                               ps[:, 4 + 2 * (b % 2):6 + 2 * (b % 2), :].rearrange("p u (k t) -> p (u k) t", k=4)
                               ).then_inc(s["stored"], 1)

            for b in range(NB):
                act.wait_ge(s["x2"], max(4, 2 * b + 2))
                act.wait_ge(s["squared"], NB + b)
                nc.scalar.activation(junk, x2[:, b, :], ACT.Square, accum_out=ss[:, b:b + 1]).then_inc(s["squared"], 1)
                act.wait_ge(s["mean"], 2 + b + 1)
                nc.scalar.activation(ss[:, 8 + b:9 + b], ss[:, 8 + b:9 + b], ACT.Sqrt).then_inc(s["root"], 1)
                if b >= 2:
                    store(b - 2)
            store(NB - 2)
            store(NB - 1)

        @block.vector
        def _(dve):
            def norm(b):
                dve.wait_ge(s["squared"], NB + b + 1)
                nc.vector.tensor_scalar(ss[:, 8 + b:9 + b], ss[:, b:b + 1], 1.0 / D, EPS, ALU.mult, ALU.add
                                        ).then_inc(s["mean"], 1)
                dve.wait_ge(s["root"], 2 + b + 1)
                nc.vector.reciprocal(ss[:, 16 + b:17 + b], ss[:, 8 + b:9 + b]).then_inc(s["rstd"], 1)
                dve.wait_ge(s["rstd"], 2 + b + 1)
                nc.vector.scalar_tensor_tensor(out=h2[:, b, :], in0=x2[:, b, :], scalar=ss[:, 16 + b:17 + b],
                                               in1=m["nrow"][:], op0=ALU.mult, op1=ALU.mult).then_inc(s["normed"], 1)

            dve.wait_ge(s["x_again"], 16)
            dve.wait_ge(s["ffn_row"], 16)
            for n, (b, c) in enumerate(order):
                part = x2[:, b, c * 512:(c + 1) * 512]
                dve.wait_ge(s["half_psum"], 32 + n + 1)
                nc.vector.tensor_tensor(part, part, ps[:, n % 4, :], ALU.add).then_inc(s["x2"], 1)
                if n == 3:
                    norm(0)
                    norm(1)
                elif n % 2 == 1 and n > 3:
                    norm(b)


def peer(nc, m, s, io):
    x2 = seg(m["A"], 0, NB, D)
    h2 = seg(m["C"], 0, NB, D)
    h2_t = seg(m["B"], 0, KT, T)
    ring = seg(m["D"], 0, RING, 2 * D)
    wq = seg(m["B"], WQ, 2, KT, P)
    q_t = seg(m["B"], QT, 2, T)
    keys = seg(m["B"], KEYS, 2, NK)
    sc = seg(m["B"], SC, 2, 2, NK)
    cand = seg(m["B"], CAND, K, K)
    cand_flat = seg(m["B"], CAND, K * K)
    onehot = seg(m["B"], ONEHOT, 2 * K, K)
    top_v = seg(m["B"], TOPV, 2, K)
    top_f = seg(m["B"], TOPF, 2, K)
    best_v = seg(m["B"], BESTV, NB, K)
    gate = seg(m["B"], GATE, NB, K)
    a_raw, a_gelu, a_gated, picked = (seg(m["B"], ACTV + 16 * i, K) for i in range(4))
    place_f = seg(m["B"], IDS, 2, K)
    picked_ids = seg(m["B"], IDS + 32, 2, K)
    gate_sum = seg(m["B"], IDS + 64, NB)
    gate_rec = seg(m["B"], IDS + 72, NB)
    ps, col = m["ps"], m["col"]
    top_i, best_i, place, ids = (handle[:] for handle in m["u32"])
    diag = seg(m["B"], DIAG, 2 * PAIR, P)
    GROUPS = K // PAIR
    HALF_K, HALF_RING = K // 2, RING // 2
    STEPS = 25
    PIECES = [(0, P), (P, T // 2), (T // 2, T)]
    PICKS = [[(0, b + 4)] for b in range(4)] + [[(1, 2 * i), (1, 2 * i + 1)] for i in range(4)]
    SCORES_AT_START = [[]] * 4 + [([(1, 0)] if i == 0 else []) + [(1, 2 * i + 1)] for i in range(4)]
    SCORES_WITHIN = [[(0, b + 5)] for b in range(3)] + [[]] + [[(1, 2 * i + 2)] for i in range(3)] + [[]]

    def piece_of(b):
        return 0 if b == 0 else 1 if b < 4 else 2

    with nc.Block() as block:
        @block.sync
        def _(sp):
            sp.dma_start(seg(m["B"], WQ, 2048), io["w_query"][0]).then_inc(s["wq"], 16)
            sp.dma_start(seg(m["B"], KEYS, 256), io["keys"][0]).then_inc(s["keys"], 16)
            with sp.Fori(0, PH - 1) as hd:
                sp.wait_ge(s["q_psum2"], 2 * hd + 3)
                sp.dma_start(seg(m["B"], WQ, 2048), io["w_query"][bass.ds(hd + 1, 1)].rearrange("a p n -> p (a n)")
                             ).then_inc(s["wq"], 16)
                sp.wait_ge(s["sc_psum"], NB * (hd + 1))
                sp.dma_start(seg(m["B"], KEYS, 256), io["keys"][bass.ds(hd + 1, 1)].rearrange("a p n -> p (a n)")
                             ).then_inc(s["keys"], 16)

        @block.tensor
        def _(pe):
            def first_products(piece, half):
                lo, hi = PIECES[piece]
                out = ps[:, 6, half * P:(half + 1) * P] if piece == 0 else ps[:, 2 * piece - 2 + half, 0:hi - lo]
                for kt in range(KT):
                    last = nc.tensor.matmul(out, wq[:, half, kt, :], h2_t[:, kt, lo:hi],
                                            start=(kt == 0), stop=(kt == KT - 1))
                if half == 1:
                    last.then_inc(s["q_psum2"], 1)

            def project_step(hd, b, i):
                half, u, kt = b // 4, b // 2 % 2, b % 2 * 4 + i
                if b == 0 and i == 0:
                    pe.wait_ge(s["wq"], 16 * (hd + 1))
                last = nc.tensor.matmul(ps[:, 2 * half + u, :], wq[:, half, kt, :],
                                        h2_t[:, kt, u * 512:(u + 1) * 512], start=(kt == 0), stop=(kt == KT - 1))
                if b % 4 == 3 and i == 3:
                    last.then_inc(s["q_psum2"], 1)

            def score(hd, b):
                if first(hd):
                    pe.wait_ge(s["q_t"], piece_of(b) + 1)
                elif b == 0:
                    pe.wait_ge(s["q_t"], 2 * hd + 3)
                if b == 0:
                    pe.wait_ge(s["keys"], 16 * (hd + 1))
                if not (first(hd) and b < 2):
                    pe.wait_ge(s["sc"], NB * hd + b - 1)
                for half in range(2):
                    last = nc.tensor.matmul(ps[:, 4 + b % 2, half * NK:(half + 1) * NK],
                                            q_t[:, half, b * P:(b + 1) * P], keys[:, half, :], start=True, stop=True)
                last.then_inc(s["sc_psum"], 1)

            def body(hd, prepare, ahead):
                for b in range(NB):
                    it = NB * hd + b
                    if first(hd):
                        for item in SCORES_AT_START[b]:
                            score(*item)
                    elif prepare and b == 0:
                        score(hd + 1, 0)
                    for q in range(GROUPS // 2):
                        if q == 0:
                            pe.wait_ge(s["expert_banks"], it + 1)
                        for i in range(PAIR):
                            n = PAIR * q + i
                            slot = PAIR * (2 * q + 1) + i
                            pe.wait_ge(s["diag_done"], it * HALF_K + n + 1)
                            for u in range(2):
                                last = nc.tensor.matmul(
                                    ps[:, 6 + u, :], diag[:, n % (2 * PAIR), :],
                                    ring[:, slot % RING, D + u * 512:D + (u + 1) * 512],
                                    start=(n == 0), stop=(n == HALF_K - 1), skip_group_check=True)
                            last.then_inc(s["slot_free_pe"], 1)
                        if first(hd):
                            for i in range(2):
                                project_step(1 + b // 4, b % 4 * 2 + q // 2, q % 2 * 2 + i)
                            if q == 1:
                                for item in SCORES_WITHIN[b]:
                                    score(*item)
                        else:
                            if ahead:
                                project_step(hd + 2, b, q)
                            if prepare and q == 1 and b + 1 < NB:
                                score(hd + 1, b + 1)
            pe.wait_ge(s["wq"], 16)
            first_products(0, 0)
            first_products(0, 1)
            first_products(1, 0)
            score(0, 0)
            first_products(1, 1)
            first_products(2, 0)
            for b in range(1, 4):
                score(0, b)
            first_products(2, 1)
            score(0, 4)
            body(0, True, True)
            with pe.Fori(1, PH - 2) as hd:
                body(hd, True, True)
            body(PH - 2, True, False)
            body(PH - 1, False, False)

        @block.gpsimd
        def _(pool):
            def item(hd, b):
                pool.wait_ge(s["ids"], NB * hd + b + 1)
                pool.sem_inc(s["gate"], 1)
                for j in range(K):
                    r = j % RING
                    owner, n = ("slot_free_pe" if j // PAIR % 2 else "slot_free"), j // (2 * PAIR) * PAIR + j % PAIR
                    pool.wait_ge(s[owner], (NB * hd + b) * HALF_K + n + 1)
                    pool.sem_inc(s["gate"], 1)
                    pool.indirect_dma_start(ring[:, r, :], None, io["experts"],
                                            bass.IndirectOffsetOnAxis(ap=ids[:, b, j:j + 1], axis=0)
                                            ).then_inc(s[f"rows{r}"], 16)
            with pool.Fori(0, PH) as hd:
                for b in range(NB):
                    item(hd, b)

        @block.scalar
        def _(act):
            def take_queries(hd):
                for half in range(2):
                    act.wait_ge(s["q_psum2"], 2 * hd + half + 2)
                    if half == 0:
                        act.wait_ge(s["sc_psum"], NB * hd)
                    nc.scalar.copy(q_t[:, half, :], ps[:, 2 * half:2 * half + 2, :].rearrange("p a b -> p (a b)")
                                   ).then_inc(s["q_t"], 1)

            def take_first_queries(piece):
                lo, hi = PIECES[piece]
                act.wait_ge(s["q_psum2"], piece + 1)
                if piece == 0:
                    src = ps[:, 6, 0:2 * P].rearrange("p (a t) -> p a t", a=2)
                else:
                    src = ps[:, 2 * piece - 2:2 * piece, 0:hi - lo]
                nc.scalar.copy(q_t[:, :, lo:hi], src).then_inc(s["q_t"], 1)

            def take_scores(hd, b):
                act.wait_ge(s["sc_psum"], NB * hd + b + 1)
                if not (first(hd) and b < 2):
                    act.wait_ge(s["ids"], NB * hd + b - 1)
                nc.scalar.copy(sc[:, b % 2, :, :], ps[:, 4 + b % 2, 0:2 * NK].rearrange("p (a k) -> p a k", a=2)
                               ).then_inc(s["sc"], 1)

            def diagonals(hd, b, g):
                it = NB * hd + b
                act.wait_ge(s["gated"], it * GROUPS + g + 1)
                for i in range(PAIR):
                    n = g // 2 * PAIR + i
                    act.wait_ge(s["slot_free_pe"], it * HALF_K + n + 1)
                    nc.scalar.activation(diag[:, n % (2 * PAIR), :], m["ident"][:], ACT.Copy,
                                         scale=a_gated[:, PAIR * g + i:PAIR * g + i + 1]).then_inc(s["diag_done"], 1)

            def gate_exp(count, lo=0, hi=NB):
                act.wait_ge(s["gate_diff"], count)
                nc.scalar.activation(gate[:, lo:hi, :], gate[:, lo:hi, :], ACT.Exp).then_inc(s["gate_exp"], 1)

            def body(hd, prepare):
                for b in range(NB):
                    if first(hd):
                        if b == 4:
                            take_queries(1)
                        for item in SCORES_AT_START[b]:
                            take_scores(*item)
                    elif b == 0 and prepare:
                        take_queries(hd + 1)
                        take_scores(hd + 1, 0)
                    for g in range(GROUPS):
                        act.wait_ge(s["dots"], (NB * hd + b) * K + PAIR * (g + 1))
                        nc.scalar.activation(a_gelu[:, PAIR * g:PAIR * (g + 1)], a_raw[:, PAIR * g:PAIR * (g + 1)],
                                             ACT.Gelu).then_inc(s["gelu"], 1)
                        if g % 2 == 1:
                            diagonals(hd, b, g)
                        if g == 6 and first(hd):
                            for item in SCORES_WITHIN[b]:
                                take_scores(*item)
                        elif g == 6 and prepare and b + 1 < NB:
                            take_scores(hd + 1, b + 1)
                    if first(hd) and b == 3:
                        gate_exp(2, 4, NB)
                if prepare:
                    gate_exp(hd + 3)
            take_first_queries(0)
            take_scores(0, 0)
            take_first_queries(1)
            for b in range(1, 4):
                take_scores(0, b)
            gate_exp(1, 0, 4)
            take_first_queries(2)
            take_scores(0, 4)
            body(0, True)
            with act.Fori(1, PH - 1) as hd:
                body(hd, True)
            body(PH - 1, False)

        @block.vector
        def _(dve):
            dve.sem_inc(s["slot_free"], HALF_RING)
            dve.sem_inc(s["slot_free_pe"], HALF_RING)
            dve.sem_inc(s["expert_banks"], 1)

            def pick(hd, b):
                done = [0]

                def step(ins):
                    ins.then_inc(s["pick"], 1)
                    done[0] += 1

                def former_steps():
                    dve.wait_ge(s["pick"], (NB * hd + b) * STEPS + done[0])
                    dve.sem_inc(s["gate"], 1)
                half_sc = [sc[:, b % 2, half, :] for half in range(2)]
                dve.wait_ge(s["sc"], NB * hd + b + 1)
                dve.sem_inc(s["gate"], 1)
                for rank in (0, 8):
                    for half in range(2):
                        step(nc.vector.max(top_v[:, half, rank:rank + 8], half_sc[half]))
                    yield
                    former_steps()
                    for half in range(2):
                        step(nc.vector.max_index(top_i[:, half, rank:rank + 8], top_v[:, half, rank:rank + 8], half_sc[half]))
                    if rank == 0:
                        for half in range(2):
                            step(nc.vector.match_replace(half_sc[half], top_v[:, half, 0:8], half_sc[half], LOWEST))
                    yield
                    former_steps()
                step(nc.vector.tensor_copy(top_f, top_i))
                step(nc.vector.tensor_tensor(cand, top_v[:, 0, :].unsqueeze(2).to_broadcast([P, K, K]),
                                             top_v[:, 1:2, :].to_broadcast([P, K, K]), ALU.add))
                yield
                former_steps()
                for rank in (0, 8):
                    step(nc.vector.max(best_v[:, b, rank:rank + 8], cand_flat))
                    yield
                    former_steps()
                    step(nc.vector.max_index(best_i[:, rank:rank + 8], best_v[:, b, rank:rank + 8], cand_flat))
                    if rank == 0:
                        step(nc.vector.match_replace(cand_flat, best_v[:, b, 0:8], cand_flat, LOWEST))
                    yield
                    former_steps()
                step(nc.vector.tensor_scalar(place[:, 0, :], best_i, 4, None, ALU.logical_shift_right))
                step(nc.vector.tensor_scalar(place[:, 1, :], best_i, 15, None, ALU.bitwise_and))
                yield
                former_steps()
                step(nc.vector.tensor_copy(place_f, place))
                yield
                former_steps()
                step(nc.vector.tensor_tensor(
                    onehot, place_f.rearrange("p a j -> p (a j)").unsqueeze(2).to_broadcast([P, 2 * K, K]),
                    col[:, IOTA:IOTA + K].unsqueeze(1).to_broadcast([P, 2 * K, K]), ALU.is_equal))
                yield
                former_steps()
                for half in range(2):
                    part = onehot[:, half * K:(half + 1) * K, :]
                    step(nc.vector.tensor_tensor(part, part, top_f[:, half:half + 1, :].to_broadcast([P, K, K]), ALU.mult))
                yield
                former_steps()
                step(nc.vector.tensor_reduce(picked_ids.rearrange("p a j -> p (a j)"), onehot, AX_X, ALU.add))
                yield
                former_steps()
                step(nc.vector.tensor_scalar(picked, picked_ids[:, 0, :], float(NK), None, ALU.mult))
                yield
                former_steps()
                nc.vector.tensor_tensor(ids[:, b, :], picked, picked_ids[:, 1, :], ALU.add).then_inc(s["ids"], 1)
                assert done[0] == STEPS

            def gates(hd, count, lo=0, hi=NB):
                part = gate[:, lo:hi, :]
                dve.wait_ge(s["ids"], NB * hd + hi)
                nc.vector.tensor_tensor(part, best_v[:, lo:hi, :], best_v[:, lo:hi, 0:1].to_broadcast([P, hi - lo, K]),
                                        ALU.subtract).then_inc(s["gate_diff"], 1)
                dve.wait_ge(s["gate_exp"], count)
                nc.vector.tensor_reduce(gate_sum[:, lo:hi], part, AX_X, ALU.add).then_inc(s["gate_sum"], 1)
                dve.wait_ge(s["gate_sum"], count)
                nc.vector.reciprocal(gate_rec[:, lo:hi], gate_sum[:, lo:hi]).then_inc(s["gate_rec"], 1)
                dve.wait_ge(s["gate_rec"], count)
                nc.vector.tensor_tensor(part, part, gate_rec[:, lo:hi].unsqueeze(2).to_broadcast([P, hi - lo, K]), ALU.mult
                                        ).then_inc(s["gates"], 1)

            def dots(hd, b, g):
                for j in range(PAIR * g, PAIR * (g + 1)):
                    use = (NB * hd + b) * (K // RING) + j // RING
                    dve.wait_ge(s[f"rows{j % RING}"], 16 * (use + 1))
                    u_rows = ring[:, j % RING, 0:D]
                    nc.vector.tensor_tensor_reduce(u_rows, u_rows, h2[:, b, :], 1.0, 0.0, ALU.mult, ALU.add,
                                                   a_raw[:, j:j + 1]).then_inc(s["dots"], 1)

            def add_experts(hd, b, g):
                it = NB * hd + b
                cols = slice(PAIR * g, PAIR * (g + 1))
                dve.wait_ge(s["gelu"], it * GROUPS + g + 1)
                nc.vector.tensor_tensor(a_gated[:, cols], a_gelu[:, cols], gate[:, b, cols], ALU.mult
                                        ).then_inc(s["gated"], 1)
                if g % 2 == 1:
                    return
                dve.wait_ge(s["gated"], it * GROUPS + g + 1)
                for j in range(PAIR * g, PAIR * (g + 1)):
                    n = g // 2 * PAIR + j % PAIR
                    dve.wait_ge(s["slot_free"], it * HALF_K + n + HALF_RING)
                    nc.vector.scalar_tensor_tensor(out=x2[:, b, :], in0=ring[:, j % RING, D:2 * D],
                                                   scalar=a_gated[:, j:j + 1], in1=x2[:, b, :],
                                                   op0=ALU.mult, op1=ALU.add).then_inc(s["slot_free"], 1)

            def add_bank_sums(hd, b):
                it = NB * hd + b
                dve.wait_ge(s["slot_free_pe"], it * HALF_K + HALF_K + HALF_RING)
                dve.wait_ge(s["slot_free"], it * HALF_K + HALF_K + HALF_RING)
                nc.vector.tensor_tensor(x2[:, b, :], x2[:, b, :], ps[:, 6:8, :].rearrange("p u n -> p (u n)"), ALU.add
                                        ).then_inc(s["expert_banks"], 1)

            def body(hd, prepare):
                if not first(hd):
                    dve.wait_ge(s["gates"], hd + 2)
                for b in range(NB):
                    if first(hd) and b % 4 == 0:
                        dve.wait_ge(s["gates"], 1 + b // 4)
                    dve.wait_ge(s["expert_banks"], NB * hd + b + 1)
                    if first(hd):
                        picking = itertools.chain(*[pick(*item) for item in PICKS[b]])
                    else:
                        picking = pick(hd + 1, b) if prepare else iter(())
                    for g in range(GROUPS):
                        dots(hd, b, g)
                        for _ in range(4 if first(hd) and b >= 4 else 2):
                            next(picking, None)
                        add_experts(hd, b, g)
                    for _ in picking:
                        pass
                    add_bank_sums(hd, b)
                    if first(hd) and b == 3:
                        gates(0, 2, 4, NB)
                if prepare:
                    gates(hd + 1, hd + 3)
            for b in range(4):
                for _ in pick(0, b):
                    pass
            gates(0, 1, 0, 4)
            body(0, True)
            with dve.Fori(1, PH - 1) as hd:
                body(hd, True)
            body(PH - 1, False)


def norm_final(nc, m, s, io):
    x2 = seg(m["A"], 0, NB, D)
    out = seg(m["C"], 0, NB, D)
    ss = m["ss"]
    with nc.Block() as block:
        @block.sync
        def _(sp):
            sp.dma_start(m["nrow"][:], io["final_row"]).then_inc(s["final_row"], 16)
            for b in range(NB):
                sp.wait_ge(s["final"], b + 1)
                sp.dma_start(io["out"][b * P:(b + 1) * P, :], out[:, b, :]).then_inc(s["written"], 16)
            sp.wait_ge(s["written"], 16 * NB)

        @block.scalar
        def _(act):
            for b in range(NB):
                nc.scalar.activation(out[:, b, :], x2[:, b, :], ACT.Square, accum_out=ss[:, b:b + 1]
                                     ).then_inc(s["squared"], 1)
            act.wait_ge(s["mean"], 11)
            nc.scalar.activation(ss[:, 8:16], ss[:, 8:16], ACT.Sqrt).then_inc(s["root"], 1)

        @block.vector
        def _(dve):
            dve.wait_ge(s["final_row"], 16)
            dve.wait_ge(s["squared"], 3 * NB)
            nc.vector.tensor_scalar(ss[:, 8:16], ss[:, 0:8], 1.0 / D, EPS, ALU.mult, ALU.add).then_inc(s["mean"], 1)
            dve.wait_ge(s["root"], 11)
            nc.vector.reciprocal(ss[:, 16:24], ss[:, 8:16]).then_inc(s["rstd"], 1)
            dve.wait_ge(s["rstd"], 11)
            for b in range(NB):
                nc.vector.scalar_tensor_tensor(out=out[:, b, :], in0=x2[:, b, :], scalar=ss[:, 16 + b:17 + b],
                                               in1=m["nrow"][:], op0=ALU.mult, op1=ALU.mult).then_inc(s["final"], 1)


def kernel(**inputs):
    import numpy as np
    import concourse.bacc as bacc
    from concourse.bass_utils import run_bass_kernel_spmd

    a = {n: np.asarray(v) for n, v in inputs.items()}
    w_in = a["w_in"][0]
    W = D

    def tiles(w, n):
        return np.ascontiguousarray(w.reshape(w.shape[0] // P, P, n, -1).transpose(2, 1, 0, 3).reshape(n, P, -1))

    def rows(v):
        return np.ascontiguousarray(np.broadcast_to(v.reshape(1, -1), (P, v.size)))

    def columns(v):
        return v.reshape(-1, P).T

    cols = np.zeros((P, TMP), np.float32)
    cols[:, LBL:LBL + 8] = columns(a["hg_lb_logits"][0])
    cols[:, LBL + 8:LBL + 16] = columns(a["hg_lb_logits"][1])
    cols[:, HGW:HGW + 1] = columns(a["hg_norm_w"][0])
    cols[:, CONVW:CONVW + CT * TAPS] = a["ssd_conv_w"][0].reshape(TAPS, CT, P).transpose(2, 1, 0).reshape(P, CT * TAPS)
    cols[:, CONVB:CONVB + CT] = columns(a["ssd_conv_b"][0])
    cols[:, SSDW:SSDW + 8] = columns(a["ssd_norm_w"][0])
    cols[0:SSD_HEADS, SSDH] = a["ssd_dt_bias"][0]
    cols[0:SSD_HEADS, SSDH + 1] = a["ssd_A_log"][0]
    cols[:, DROW:DROW + SSD_HEADS] = rows(a["ssd_D"][0])
    cols[:, IOTA:IOTA + K] = np.arange(K)
    t = np.arange(P)
    sel = np.zeros((SSD_HEADS, SSD_HEADS, P), np.float32)
    sel[np.arange(SSD_HEADS), np.arange(SSD_HEADS)] = 1
    keep = np.ones((P, T), np.float32)
    keep[:, ::C] = 0
    arrays = {
        "x": np.ascontiguousarray(a["x"][0]),
        "norm_mix_row": rows(a["norm_mix_w"][0]),
        "norm_ffn_row": rows(a["norm_ffn_w"][0]),
        "final_row": rows(a["final_norm_w"]),
        "cols": cols,
        "ident": np.eye(P, dtype=np.float32),
        "mask": ((t[:, None] <= t[None, :]) & (t[:, None] // C == t[None, :] // C)).astype(np.uint32),
        "keep": keep,
        "sel": sel.reshape(SSD_HEADS, -1),
        "w_v": tiles(w_in[:, 2 * W:3 * W], 2),
        "w_hg": np.ascontiguousarray(np.concatenate([tiles(w_in[:, W:2 * W], 8), tiles(w_in[:, 3 * W:4 * W], 8),
                                                     tiles(w_in[:, 0:W], 8)], axis=2)),
        "w_z": tiles(w_in[:, 4 * W:5 * W], 2),
        "w_xbc": tiles(w_in[:, 5 * W:5 * W + CT * P], CT),
        "w_dt": tiles(w_in[:, 5 * W + CT * P:], 1)[0],
        "w_out": tiles(a["w_out"][0], 2),
        "w_query": np.ascontiguousarray(tiles(a["peer_w_q"][0], 16).reshape(PH, 2, P, D).transpose(0, 2, 1, 3).reshape(PH, P, 2 * D)),
        "keys": np.ascontiguousarray(a["peer_keys"][0].transpose(0, 3, 1, 2).reshape(PH, P, 2 * NK)),
        "experts": np.concatenate([a["peer_u"][0], a["peer_v"][0]], axis=1),
    }
    nc = bacc.Bacc("TRN2", target_bir_lowering=False, num_devices=1)
    io = {n: nc.dram_tensor("in_" + n, v.shape, mybir.dt.from_np(v.dtype), kind="ExternalInput").ap()
          for n, v in arrays.items()}
    out = nc.dram_tensor("out_x", (1, T, D), F32, kind="ExternalOutput").ap()
    io["out"] = out.rearrange("a t d -> (a t) d")
    layer(nc, io)
    r = run_bass_kernel_spmd(nc, [{"in_" + n: v for n, v in arrays.items()}], core_ids=[0])
    return r.results[0]["out_x"]
```
